# Optimizing a Trainium2 kernel written in Bass

```python
import math
import jax, jax.numpy as jnp
from jax import lax
import numpy as np

D_MODEL = 1024
BATCH = 1
SEQ = 256
DEPTH = 2

D_MIX = D_MODEL
DN_HEADS = 4
DN_HEAD_DIM = 128
DN_WIDTH = DN_HEADS * DN_HEAD_DIM
DN_CONV = 4
CHUNK = 64
SC_WIDTH = D_MIX - DN_WIDTH
SC_GROUPS = 4
SC_GROUP_DIM = SC_WIDTH // SC_GROUPS
SC_CONV = 3
D_FF = ((8 * D_MODEL + 3 * 256 - 1) // (3 * 256)) * 256
W_IN_COLS = 4 * DN_WIDTH + 2 * DN_HEADS + 3 * SC_WIDTH
EPS = 1e-6


def rms_norm(x, gain):
    xf = x.astype(jnp.float32)
    y = xf * lax.rsqrt(jnp.mean(xf * xf, axis=-1, keepdims=True) + EPS)
    return (y * gain.astype(jnp.float32)).astype(x.dtype)

def l2_normalize(x):
    return x * lax.rsqrt(jnp.sum(x * x, axis=-1, keepdims=True) + EPS)

def causal_depthwise_conv(x, w):
    K = w.shape[0]
    T = x.shape[1]
    xp = jnp.pad(x, ((0, 0), (K - 1, 0), (0, 0)))
    y = xp[:, 0:T, :] * w[0]
    for j in range(1, K):
        y = y + xp[:, j:j + T, :] * w[j]
    return y

def chunk_gated_delta_rule(q, k, v, g, beta):
    Bsz, T, H, DK = q.shape
    DV = v.shape[-1]
    C = CHUNK
    N = T // C
    q = q * (DK ** -0.5)

    def to_chunks(t):
        return t.reshape(Bsz, N, C, H, t.shape[-1]).transpose(0, 3, 1, 2, 4)

    q, k, v = to_chunks(q), to_chunks(k), to_chunks(v)
    g = jnp.cumsum(g.reshape(Bsz, N, C, H).transpose(0, 3, 1, 2), axis=-1)
    beta = beta.reshape(Bsz, N, C, H).transpose(0, 3, 1, 2)

    causal = jnp.tril(jnp.ones((C, C), dtype=bool))
    strict = jnp.tril(jnp.ones((C, C), dtype=bool), -1)
    decay = jnp.exp(jnp.where(causal, g[..., :, None] - g[..., None, :], -jnp.inf))

    k_beta = k * beta[..., None]
    v_beta = v * beta[..., None]
    lower = jnp.where(strict, jnp.einsum('bhncd,bhnmd->bhncm', k_beta, k) * decay, 0.0)
    a_mat = lower + jnp.eye(C, dtype=jnp.float32)
    rhs = jnp.concatenate([v_beta, k_beta * jnp.exp(g)[..., None]], axis=-1)
    sol = lax.linalg.triangular_solve(a_mat, rhs, left_side=True, lower=True, unit_diagonal=True)
    u, w = sol[..., :DV], sol[..., DV:]

    qk = jnp.einsum('bhncd,bhnmd->bhncm', q, k) * decay
    q_dec = q * jnp.exp(g)[..., None]
    k_dec = k * jnp.exp(g[..., -1:] - g)[..., None]
    g_last = jnp.exp(g[..., -1])

    def step(S, xs):
        qk_i, q_dec_i, k_dec_i, u_i, w_i, gl_i = xs
        v_new = u_i - jnp.einsum('bhck,bhkv->bhcv', w_i, S)
        o_i = jnp.einsum('bhck,bhkv->bhcv', q_dec_i, S) + jnp.einsum('bhcm,bhmv->bhcv', qk_i, v_new)
        S = S * gl_i[..., None, None] + jnp.einsum('bhck,bhcv->bhkv', k_dec_i, v_new)
        return S, o_i

    xs = (jnp.moveaxis(qk, 2, 0), jnp.moveaxis(q_dec, 2, 0), jnp.moveaxis(k_dec, 2, 0),
          jnp.moveaxis(u, 2, 0), jnp.moveaxis(w, 2, 0), jnp.moveaxis(g_last, 2, 0))
    S0 = jnp.zeros((Bsz, H, DK, DV), dtype=jnp.float32)
    _, o = lax.scan(step, S0, xs)
    return o.transpose(1, 0, 3, 2, 4).reshape(Bsz, T, H, DV)

def hybrid_layer(x, norm1_g, w_in, dn_conv_w, dn_a_log, dn_dt_bias, dn_norm_g,
                 sc_conv_w, sc_norm_g, w_out, norm2_g, ffn_w_gate, ffn_w_up, ffn_w_down):
    Bsz, T, _ = x.shape
    h = rms_norm(x, norm1_g)
    proj = h @ w_in
    o1 = 3 * DN_WIDTH
    o2 = o1 + DN_WIDTH
    o3 = o2 + DN_HEADS
    o4 = o3 + DN_HEADS
    qkv, z, b_in, a_in, sc_in = proj[..., :o1], proj[..., o1:o2], proj[..., o2:o3], proj[..., o3:o4], proj[..., o4:]

    qkv = jax.nn.silu(causal_depthwise_conv(qkv, dn_conv_w)).astype(jnp.float32)
    q = l2_normalize(qkv[..., :DN_WIDTH].reshape(Bsz, T, DN_HEADS, DN_HEAD_DIM))
    k = l2_normalize(qkv[..., DN_WIDTH:2 * DN_WIDTH].reshape(Bsz, T, DN_HEADS, DN_HEAD_DIM))
    v = qkv[..., 2 * DN_WIDTH:].reshape(Bsz, T, DN_HEADS, DN_HEAD_DIM)
    beta = jax.nn.sigmoid(b_in.astype(jnp.float32))
    g = -jnp.exp(dn_a_log.astype(jnp.float32)) * jax.nn.softplus(
        a_in.astype(jnp.float32) + dn_dt_bias.astype(jnp.float32))
    o_dn = chunk_gated_delta_rule(q, k, v, g, beta)
    zf = z.astype(jnp.float32).reshape(Bsz, T, DN_HEADS, DN_HEAD_DIM)
    o_dn = (o_dn * lax.rsqrt(jnp.mean(o_dn * o_dn, axis=-1, keepdims=True) + EPS)
            * dn_norm_g.astype(jnp.float32) * jax.nn.silu(zf))
    o_dn = o_dn.reshape(Bsz, T, DN_WIDTH).astype(x.dtype)

    gate_b, gate_c, hv = sc_in[..., :SC_WIDTH], sc_in[..., SC_WIDTH:2 * SC_WIDTH], sc_in[..., 2 * SC_WIDTH:]
    y = gate_b * causal_depthwise_conv(gate_c * hv, sc_conv_w)
    yf = y.astype(jnp.float32).reshape(Bsz, T, SC_GROUPS, SC_GROUP_DIM)
    yf = yf * lax.rsqrt(jnp.mean(yf * yf, axis=-1, keepdims=True) + EPS)
    o_sc = (yf * sc_norm_g.astype(jnp.float32).reshape(SC_GROUPS, SC_GROUP_DIM)).reshape(Bsz, T, SC_WIDTH).astype(x.dtype)

    x = x + jnp.concatenate([o_dn, o_sc], axis=-1) @ w_out

    h2 = rms_norm(x, norm2_g)
    x = x + (jax.nn.silu(h2 @ ffn_w_gate) * (h2 @ ffn_w_up)) @ ffn_w_down
    return x

def first_inputs(seed: int = 0) -> dict:
    key = jax.random.key(seed)
    ks = jax.random.split(key, 16)
    f32 = jnp.float32

    def nrm(k, shape, scale):
        return jax.random.normal(k, shape, f32) * scale

    def gain(k, shape):
        return 1.0 + 0.02 * jax.random.normal(k, shape, f32)

    x = nrm(ks[0], (BATCH, SEQ, D_MODEL), 1.0)
    norm1_g = gain(ks[1], (DEPTH, D_MODEL))
    w_in = nrm(ks[2], (DEPTH, D_MODEL, W_IN_COLS), D_MODEL ** -0.5)
    dn_conv_w = nrm(ks[3], (DEPTH, DN_CONV, 3 * DN_WIDTH), DN_CONV ** -0.5)
    dn_a_log = jnp.log(jax.random.uniform(ks[4], (DEPTH, DN_HEADS), f32, 1.0, 16.0))
    dt = jnp.exp(jax.random.uniform(ks[5], (DEPTH, DN_HEADS), f32, math.log(1e-3), math.log(1e-1)))
    dn_dt_bias = dt + jnp.log(-jnp.expm1(-dt))
    dn_norm_g = gain(ks[6], (DEPTH, DN_HEAD_DIM))
    sc_conv_w = nrm(ks[7], (DEPTH, SC_CONV, SC_WIDTH), SC_CONV ** -0.5)
    sc_norm_g = gain(ks[8], (DEPTH, SC_WIDTH))
    w_out = nrm(ks[9], (DEPTH, D_MIX, D_MODEL), D_MIX ** -0.5)
    norm2_g = gain(ks[10], (DEPTH, D_MODEL))
    ffn_w_gate = nrm(ks[11], (DEPTH, D_MODEL, D_FF), D_MODEL ** -0.5)
    ffn_w_up = nrm(ks[12], (DEPTH, D_MODEL, D_FF), D_MODEL ** -0.5)
    ffn_w_down = nrm(ks[13], (DEPTH, D_FF, D_MODEL), D_FF ** -0.5)
    final_norm_g = gain(ks[14], (D_MODEL,))
    return {'x': x, 'norm1_g': norm1_g, 'w_in': w_in, 'dn_conv_w': dn_conv_w,
            'dn_a_log': dn_a_log, 'dn_dt_bias': dn_dt_bias, 'dn_norm_g': dn_norm_g,
            'sc_conv_w': sc_conv_w, 'sc_norm_g': sc_norm_g, 'w_out': w_out,
            'norm2_g': norm2_g, 'ffn_w_gate': ffn_w_gate, 'ffn_w_up': ffn_w_up,
            'ffn_w_down': ffn_w_down, 'final_norm_g': final_norm_g}

def first_block(x, norm1_g, w_in, dn_conv_w, dn_a_log, dn_dt_bias, dn_norm_g, sc_conv_w,
              sc_norm_g, w_out, norm2_g, ffn_w_gate, ffn_w_up, ffn_w_down, final_norm_g):
    for l in range(DEPTH):
        x = hybrid_layer(x, norm1_g[l], w_in[l], dn_conv_w[l], dn_a_log[l], dn_dt_bias[l],
                         dn_norm_g[l], sc_conv_w[l], sc_norm_g[l], w_out[l], norm2_g[l],
                         ffn_w_gate[l], ffn_w_up[l], ffn_w_down[l])
    return rms_norm(x, final_norm_g)


SSM_WIDTH = 512
SSM_GROUP = 16
SSM_GROUPS = SSM_WIDTH // SSM_GROUP
SSM_STATE = 64
LOG_DT_MIN = math.log(1e-3)
LOG_DT_MAX = math.log(1e-1)
ATTN_HEADS = 8
HEAD_DIM = 64
ATTN_WIDTH = ATTN_HEADS * HEAD_DIM
Q_BLOCK = 128
D_FF_2 = 2816
FFN_RES = 0.5
N_SUB = 3
RMS_EPS = 1e-6
IN_WIDTH = SSM_WIDTH + 3 * ATTN_WIDTH + ATTN_HEADS + 2 * D_MODEL


def rms_norm_2(x, g):
    xf = x.astype(jnp.float32)
    xf = xf * lax.rsqrt(jnp.mean(xf * xf, axis=-1, keepdims=True) + RMS_EPS)
    return (xf * g.astype(jnp.float32)).astype(x.dtype)

def swiglu(h, w_in, w_out):
    gate, up = jnp.split(h @ w_in, 2, axis=-1)
    return (jax.nn.silu(gate) * up) @ w_out

def s5_ssm(u, a_re, a_im, log_dt, b_re, b_im, c_re, c_im, d_skip):
    f32 = jnp.float32
    bsz, L, _ = u.shape
    uf = u.astype(f32).reshape(bsz, L, SSM_GROUPS, SSM_GROUP)
    lam = lax.complex(jnp.minimum(a_re.astype(f32), -1e-4), a_im.astype(f32))
    dt = jnp.exp(log_dt.astype(f32))[:, None]
    lam_bar = jnp.exp(lam * dt)
    b = lax.complex(b_re.astype(f32), b_im.astype(f32))
    b_bar = ((lam_bar - 1.0) / lam)[..., None] * b
    bu = jnp.einsum('blgn,gpn->blgp', uf.astype(jnp.complex64), b_bar)
    a_all = jnp.broadcast_to(lam_bar, bu.shape)

    def combine(e1, e2):
        a1, s1 = e1
        a2, s2 = e2
        return a2 * a1, a2 * s1 + s2

    _, states = lax.associative_scan(combine, (a_all, bu), axis=1)
    c = lax.complex(c_re.astype(f32), c_im.astype(f32))
    y = jnp.real(jnp.einsum('gnp,blgp->blgn', c, states))
    y = y + d_skip.astype(f32).reshape(SSM_GROUPS, SSM_GROUP) * uf
    return y.reshape(bsz, L, SSM_WIDTH).astype(u.dtype)

def forgetting_attention(q, k, v, f_logit):
    f32 = jnp.float32
    bsz, L, H, Dh = q.shape
    nb = L // Q_BLOCK
    log_f = jax.nn.log_sigmoid(f_logit.astype(f32))
    cum = jnp.cumsum(log_f, axis=1).transpose(0, 2, 1)
    kt = k.transpose(0, 2, 1, 3)
    vt = v.transpose(0, 2, 1, 3)
    qb = q.transpose(0, 2, 1, 3).reshape(bsz, H, nb, Q_BLOCK, Dh).transpose(2, 0, 1, 3, 4)
    cqb = cum.reshape(bsz, H, nb, Q_BLOCK).transpose(2, 0, 1, 3)
    starts = jnp.arange(nb, dtype=jnp.int32) * Q_BLOCK
    k_pos = jnp.arange(L, dtype=jnp.int32)
    scale = Dh ** -0.5

    def one_block(args):
        q_blk, cq_blk, start = args
        s = jnp.einsum('bhqd,bhkd->bhqk', q_blk, kt).astype(f32) * scale
        s = s + (cq_blk[..., None] - cum[:, :, None, :])
        q_pos = start + jnp.arange(Q_BLOCK, dtype=jnp.int32)
        s = jnp.where(k_pos[None, :] <= q_pos[:, None], s, -jnp.inf)
        p = jax.nn.softmax(s, axis=-1).astype(vt.dtype)
        return jnp.einsum('bhqk,bhkd->bhqd', p, vt)

    out = lax.map(one_block, (qb, cqb, starts))
    return out.transpose(1, 0, 3, 2, 4).reshape(bsz, L, H * Dh)

def token_mixer(h, w_in, forget_b, a_re, a_im, log_dt, b_re, b_im, c_re, c_im,
                d_skip, glu_w, attn_w_out, w_out):
    bsz, L, _ = h.shape
    proj = h @ w_in
    cuts = np.cumsum([SSM_WIDTH, ATTN_WIDTH, ATTN_WIDTH, ATTN_WIDTH, ATTN_HEADS, D_MODEL]).tolist()
    u, q, k, v, f, g_a, g_b = jnp.split(proj, cuts, axis=-1)
    y_ssm = s5_ssm(u, a_re, a_im, log_dt, b_re, b_im, c_re, c_im, d_skip)
    z_val, z_gate = jnp.split(jax.nn.gelu(y_ssm) @ glu_w, 2, axis=-1)
    y_a = z_val * jax.nn.sigmoid(z_gate)
    shp = (bsz, L, ATTN_HEADS, HEAD_DIM)
    attn = forgetting_attention(q.reshape(shp), k.reshape(shp), v.reshape(shp), f + forget_b)
    y_b = attn @ attn_w_out
    merged = jax.nn.sigmoid(g_a) * y_a + jax.nn.sigmoid(g_b) * y_b
    return merged @ w_out

def second_inputs(seed: int = 0) -> dict:
    key = jax.random.key(seed)
    ks = jax.random.split(key, 24)
    f32 = jnp.float32
    nrm = lambda k, shape, s: jax.random.normal(k, shape, f32) * s
    D, G, P, N = D_MODEL, SSM_GROUPS, SSM_STATE, SSM_GROUP
    a_im_init = jnp.pi * jnp.arange(P, dtype=f32)
    return {
        "x": nrm(ks[0], (BATCH, SEQ, D), 1.0),
        "c": nrm(ks[1], (BATCH, D), 1.0),
        "mod_w": nrm(ks[2], (DEPTH, D, N_SUB * 3 * D), 0.5 * D ** -0.5),
        "mod_b": nrm(ks[3], (DEPTH, N_SUB * 3 * D), 0.01),
        "norm_pre": 1.0 + nrm(ks[4], (DEPTH, N_SUB, D), 0.02),
        "norm_post": 1.0 + nrm(ks[5], (DEPTH, N_SUB, D), 0.02),
        "ffn_w_in": nrm(ks[6], (DEPTH, 2, D, 2 * D_FF_2), D ** -0.5),
        "ffn_w_out": nrm(ks[7], (DEPTH, 2, D_FF_2, D), D_FF_2 ** -0.5),
        "mix_w_in": nrm(ks[8], (DEPTH, D, IN_WIDTH), D ** -0.5),
        "forget_b": 3.0 + nrm(ks[9], (DEPTH, ATTN_HEADS), 0.5),
        "ssm_a_re": -0.5 + nrm(ks[10], (DEPTH, G, P), 0.01),
        "ssm_a_im": a_im_init + nrm(ks[11], (DEPTH, G, P), 0.01),
        "ssm_log_dt": jax.random.uniform(ks[12], (DEPTH, G), f32, LOG_DT_MIN, LOG_DT_MAX),
        "ssm_b_re": nrm(ks[13], (DEPTH, G, P, N), (2 * N) ** -0.5),
        "ssm_b_im": nrm(ks[14], (DEPTH, G, P, N), (2 * N) ** -0.5),
        "ssm_c_re": nrm(ks[15], (DEPTH, G, N, P), (2 * P) ** -0.5),
        "ssm_c_im": nrm(ks[16], (DEPTH, G, N, P), (2 * P) ** -0.5),
        "ssm_d": nrm(ks[17], (DEPTH, SSM_WIDTH), 1.0),
        "glu_w": nrm(ks[18], (DEPTH, SSM_WIDTH, 2 * D), SSM_WIDTH ** -0.5),
        "attn_w_out": nrm(ks[19], (DEPTH, ATTN_WIDTH, D), ATTN_WIDTH ** -0.5),
        "mix_w_out": nrm(ks[20], (DEPTH, D, D), D ** -0.5),
    }

def second_block(x, c, mod_w, mod_b, norm_pre, norm_post, ffn_w_in, ffn_w_out,
              mix_w_in, forget_b, ssm_a_re, ssm_a_im, ssm_log_dt, ssm_b_re,
              ssm_b_im, ssm_c_re, ssm_c_im, ssm_d, glu_w, attn_w_out, mix_w_out):
    bsz = x.shape[0]
    for l in range(DEPTH):
        mod = (jax.nn.silu(c) @ mod_w[l] + mod_b[l]).reshape(bsz, N_SUB, 3, D_MODEL)
        mod = mod[:, :, :, None, :]

        def pre(x_in, i):
            return rms_norm_2(x_in, norm_pre[l, i]) * (1.0 + mod[:, i, 1]) + mod[:, i, 0]

        def post_add(x_in, y, i, res_w):
            return x_in + res_w * mod[:, i, 2] * rms_norm_2(y, norm_post[l, i])

        x = post_add(x, swiglu(pre(x, 0), ffn_w_in[l, 0], ffn_w_out[l, 0]), 0, FFN_RES)
        y = token_mixer(pre(x, 1), mix_w_in[l], forget_b[l], ssm_a_re[l], ssm_a_im[l],
                        ssm_log_dt[l], ssm_b_re[l], ssm_b_im[l], ssm_c_re[l], ssm_c_im[l],
                        ssm_d[l], glu_w[l], attn_w_out[l], mix_w_out[l])
        x = post_add(x, y, 1, 1.0)
        x = post_add(x, swiglu(pre(x, 2), ffn_w_in[l, 1], ffn_w_out[l, 1]), 2, FFN_RES)
    return x


def setup_inputs(seed=0):
    out = dict(first_inputs(seed))
    for name, value in second_inputs(seed + 1).items():
        if name != "x":
            out[name + "_2"] = value
    return out


def reference(
    x, norm1_g, w_in, dn_conv_w, dn_a_log, dn_dt_bias, dn_norm_g, sc_conv_w, sc_norm_g, w_out,
    norm2_g, ffn_w_gate, ffn_w_up, ffn_w_down, final_norm_g, c_2, mod_w_2, mod_b_2, norm_pre_2,
    norm_post_2, ffn_w_in_2, ffn_w_out_2, mix_w_in_2, forget_b_2, ssm_a_re_2, ssm_a_im_2,
    ssm_log_dt_2, ssm_b_re_2, ssm_b_im_2, ssm_c_re_2, ssm_c_im_2, ssm_d_2, glu_w_2,
    attn_w_out_2, mix_w_out_2,
):
    x = first_block(
        x, norm1_g, w_in, dn_conv_w, dn_a_log, dn_dt_bias, dn_norm_g, sc_conv_w, sc_norm_g,
        w_out, norm2_g, ffn_w_gate, ffn_w_up, ffn_w_down, final_norm_g,
    )
    return second_block(
        x, c_2, mod_w_2, mod_b_2, norm_pre_2, norm_post_2, ffn_w_in_2, ffn_w_out_2, mix_w_in_2,
        forget_b_2, ssm_a_re_2, ssm_a_im_2, ssm_log_dt_2, ssm_b_re_2, ssm_b_im_2, ssm_c_re_2,
        ssm_c_im_2, ssm_d_2, glu_w_2, attn_w_out_2, mix_w_out_2,
    )


_drawn_inputs = setup_inputs


def setup_inputs(seed=0):
    import zlib

    import numpy as np

    out = dict(_drawn_inputs(seed))
    spreads = {}
    factors = {'dn_norm_g': 4.811,
     'sc_norm_g': 3.056,
     'norm2_g': 2.866,
     'final_norm_g': 2.678,
     'mod_b_2': 2.916,
     'norm_pre_2': 4.31,
     'norm_post_2': 5.662,
     'ssm_a_re_2': 64.0,
     'ssm_a_im_2': 25.024,
     'ssm_log_dt_2': 200.0,
     'ssm_b_re_2': 34.872,
     'ssm_b_im_2': 34.504,
     'ssm_c_re_2': 200.0,
     'ssm_c_im_2': 200.0}
    for name, (base, spread) in spreads.items():
        noise = np.random.default_rng([zlib.crc32(name.encode()), seed]).standard_normal(out[name].shape)
        drawn = base * np.exp(spread * noise) if base else spread * noise
        out[name] = __import__('jax').numpy.asarray(drawn.astype(out[name].dtype))
    for name, factor in factors.items():
        out[name] = (out[name] * factor).astype(out[name].dtype)
    return out
```

```python
from contextlib import ExitStack

import numpy as np

import concourse.bass as bass
from concourse import mybir

F32 = mybir.dt.float32
F32R = mybir.dt.float32r
ALU = mybir.AluOpType
ACT = mybir.ActivationFunctionType
AX = mybir.AxisListType

P = 128
T = 256
TT = T // P
D = 1024
DT = D // P
LAYERS = 2
EPS = 1e-6
HEADS, HD = 4, 128
TAPS, STAPS = 4, 3
AH, AD = 8, 64
SG, SN, SP_ = 32, 16, 64
ST = SG * SP_ // P
FT = 2816 // P
MODT = 72
BIG = 1e30
ROUND = 12582912.0

UNIT = 8 * P
RAWS = 3
SLOTS = 4

def ffn_order():
    out = [("gu", 0), ("gu", 1)]
    for j in range(FT // 2):
        if 2 * j + 2 < FT:
            out.append(("gu", 2 * j + 2))
        out.append(("down", j))
        if 2 * j + 3 < FT:
            out.append(("gu", 2 * j + 3))
    return out


WEIGHTY = ("pair", "out", "gu", "down")


def with_mod(steps, weighty):
    n, done, out = sum(s[0] in weighty for s in steps), 0, []
    seen = 0
    for s in steps:
        out.append(s)
        if s[0] in weighty:
            seen += 1
            while done < (MODT // 2) * seen // n:
                out.append(("mod", done))
                done += 1
    return out


WEIGHTY = ("pair", "out", "gu", "down", "mod", "aout", "glu", "mout")

FIRST = with_mod(
    [("norm", 0), ("gates", 0), ("pair", 0), ("decay", 0), ("pair", 1), ("brow", 0), ("pair", 2), ("pair", 3),
     ("pair", 4), ("pair", 5), ("qknorm", 0), ("pair", 6), ("kk", 0), ("pair", 7), ("tok", 0), ("level", 0)]
    + [s for i in range(6) for s in (("pair", 8 + i), ("level", i + 1))]
    + [("scan", 0), ("headnorm", 0)]
    + [("out", j) for j in range(DT // 2)] + [("norm", 1)] + ffn_order() + [("acc", 0)], WEIGHTY)

SECOND = (
    [("mods", 0), ("pre", 0)] + ffn_order()[:8] + [("coef", 0)] + ffn_order()[8:]
    + [("post", 0), ("pre", 1), ("pair", 0), ("pair", 1)]
    + [s for i in range(14) for s in (("ssm", i), ("pair", 2 + i))] + [("ssm", 14), ("ssm", 15), ("gelu", 0)]
    + [("forget", 0), ("vtok", 0)] + [("head", h) for h in range(AH)]
    + [("aout", j) for j in range(4)] + [("glu", i) for i in range(DT)]
    + [("mout", j) for j in range(DT // 2)] + [("post", 1), ("pre", 2)] + ffn_order() + [("post", 2)]
)
STEPS = [(1, L, kind, i) for L in range(LAYERS) for kind, i in FIRST] + \
        [(1, LAYERS - 1, "final", 0)] + \
        [(2, L, kind, i) for L in range(LAYERS) for kind, i in SECOND]
UNITS_OF = {"pair": 2, "out": 2, "mout": 2, "gu": 2, "down": 2, "aout": 1, "glu": 1}


def numbered():
    n = dict(split=0, pair=0, norm=0, h=0, g=0, gt=0, sq=0, x=0, y=0, mod=0)
    out = []
    for B, L, kind, i in STEPS:
        out.append((B, L, kind, i, dict(n)))
        n["mod"] += kind == "mod"
        n["split"] += UNITS_OF.get(kind, 0)
        n["pair"] += kind in ("pair", "out", "mout", "gu", "aout", "glu")
        n["norm"] += kind in ("norm", "pre", "post", "final")
        n["h"] += {"norm": 8, "pre": 8, "headnorm": 8, "glu": 1}.get(kind, 4 if (kind, i) == ("head", AH - 1) else 0)
        n["g"] += {"gu": 1, "gelu": 4}.get(kind, 0)
        n["gt"] += kind in ("gu", "glu")
        n["sq"] += 4 if kind in ("norm", "pre", "post", "final", "qknorm", "headnorm") else 0
        n["x"] += {"acc": 4, "post": 8, "final": 8}.get(kind, 0)
        n["y"] += 4 if kind == "post" and i != 1 else 0
    return out, n


NUMBERED, TOTAL = numbered()
AT = {(B, L, kind, i): n for B, L, kind, i, n in NUMBERED}


def columns(sizes):
    at, out = 0, {}
    for name, n in sizes:
        out[name] = (at, at + n)
        at += n
    return out, at


P1, N1 = columns([("norm1", 8), ("norm2", 8), ("conv", 12 * TAPS), ("sconv", 4 * STAPS), ("dn_g", 1), ("sc_g", 4),
                  ("w_ba", 8 * 8), ("dt_bias", 4), ("a_log", 4), ("mod_b", MODT)])
P2, N2 = columns([("pre", 24), ("post", 24), ("w_f", 8 * 8), ("f_b", 8), ("a_re", ST), ("a_im", ST), ("log_dt", ST),
                  ("d", 4), ("b_re", 4 * P), ("b_im", 4 * P), ("c_re", ST * 32), ("c_im", ST * 32)])
PC, NC = columns([("ident", P), ("triu", P), ("ones", P), ("m", 7 * P), ("pen", 3 * P), ("time", T), ("c", 8),
                  ("final", 8)])
MXN = 18620


def build(nc, w, x_in, const_in, p1_in, p2_in, out):
    with ExitStack() as ctx:
        def sb(name, shape, dt=F32):
            return ctx.enter_context(nc.sbuf_tensor(name, shape, dt))

        def ps(name, shape):
            return ctx.enter_context(nc.psum_tensor(name, shape, F32))

        def sem(name):
            return ctx.enter_context(nc.semaphore(name))

        raw = sb("raw", [P, RAWS, 2 * UNIT])
        w_hi = sb("w_hi", [P, SLOTS, UNIT], F32R)
        w_lo = sb("w_lo", [P, SLOTS, UNIT], F32R)
        x = sb("x", [P, DT, T])
        hf = sb("hf", [P, DT, T])
        h_hi = sb("h_hi", [P, DT, T], F32R)
        h_lo = sb("h_lo", [P, DT, T], F32R)
        g_hi = sb("g_hi", [P, 4, T], F32R)
        g_lo = sb("g_lo", [P, 4, T], F32R)
        hid = sb("hid", [P, 2, T])
        gate_t = sb("gate_t", [P, 2, T])
        sq = sb("sq", [P, 2, 2 * T])
        rstd = sb("rstd", [P, T])
        std = sb("std", [P, T])
        con = sb("con", [P, NC])
        par1 = sb("par1", [P, LAYERS, N1])
        par2 = sb("par2", [P, LAYERS, N2])
        modv = sb("modv", [P, LAYERS, 3, 3, DT])
        csil = sb("csil", [P, 2, DT])
        mx = sb("mx", [P, MXN])

        stream = [ps(f"stream{i}", [P, 2, T]) for i in range(2)]
        work = [ps(f"work{i}", [P, 512]) for i in range(4)]
        stat = ps("stat", [P, 512])
        modp = ps("modp", [P, 512])

        def view(tensor, cols, name, lo, hi):
            a, b = cols[name]
            return tensor[:, a + lo:(b if hi is None else a + hi)]

        def c_(name, lo=0, hi=None):
            return view(con, PC, name, lo, hi)

        def p1_(L, name, lo=0, hi=None):
            return view(par1[:, L, :], P1, name, lo, hi)

        def p2_(L, name, lo=0, hi=None):
            return view(par2[:, L, :], P2, name, lo, hi)

        ident, triu, ones = c_("ident"), c_("triu"), c_("ones")
        triu_ones = con[:, PC["triu"][0]:PC["ones"][1]]

        def carve(whole, sizes, limit):
            cols, n = columns(sizes)
            assert n <= limit, (n, limit)
            return {k: whole[:, a:b] for k, (a, b) in cols.items()}

        A = carve(mx, [("q", 1024), ("k", 1024), ("v", 1024), ("rawp", 2 * 2 * 259), ("y", 1024), ("th", 1024),
                       ("z", 1024), ("scp", 4 * 258), ("sc", 1024), ("dec", 1024), ("lt", 1024), ("qk", 1024),
                       ("xt", 1024), ("x", 1024), ("lts", 1024), ("t", 1024), ("kd", 1024), ("vb", 1024),
                       ("small", 160)], MXN)
        qT, kT, vT, yv, th, zs, sc = (A[k].rearrange("p (n t) -> p n t", t=T) for k in
                                      ("q", "k", "v", "y", "th", "z", "sc"))
        dec, lt, qk, xt, xi, lts, tt, kd, vb = (A[k].rearrange("p (n t) -> p n t", t=P) for k in
                                                ("dec", "lt", "qk", "xt", "x", "lts", "t", "kd", "vb"))
        rawp = A["rawp"].rearrange("p (b i t) -> p b i t", b=2, i=2)
        scp = A["scp"].rearrange("p (n t) -> p n t", n=4)
        egr = A["x"][:, 0:512]
        qdec = A["y"][:, 0:512].rearrange("p (n t) -> p n t", t=P)
        sd = [A["t"][:, 0:512], A["t"][:, 512:1024], A["kd"][:, 0:512], A["kd"][:, 512:1024]]
        vn0, s_sb = lts[:, 0:4, :], lts[:, 4:8, :]
        w_sb, vn1 = tt[:, 0:4, :], tt[:, 4:8, :]
        sm = carve(A["small"], [("ba", 16), ("ap", 8), ("tb", 8), ("beta", 8), ("hb", 8), ("ab", 8), ("ln", 8),
                                ("ea", 4), ("g", 8), ("gc", 16), ("eg", 8), ("ekd", 8), ("d", 8), ("bke", 8),
                                ("sp", 8)], 160)

        Bx = carve(mx, [("u", 1024), ("q", 1024), ("k", 1024), ("v", 1024), ("sga", 2048), ("sgb", 2048),
                        ("tab", 1536), ("arg", 512), ("rnd", 512), ("bu", 1024), ("pa", 512), ("pb", 512), ("pc", 512),
                        ("pd", 512), ("z", 512), ("wv", 1024), ("s", 1024), ("cp", 1024), ("small", 500)], MXN)
        u2, q2, k2, v2, sga, sgb = (Bx[k].rearrange("p (n t) -> p n t", t=T) for k in
                                    ("u", "q", "k", "v", "sga", "sgb"))
        tab = Bx["tab"].rearrange("p (b n) -> p b n", b=2)
        bu, wv, sst = (Bx[k].rearrange("p (b n) -> p b n", b=2) for k in ("bu", "wv", "s"))
        cp = Bx["cp"].rearrange("p (b s n) -> p b s n", b=2, n=32)
        a0, b0 = columns([("u", 1024), ("q", 1024), ("k", 1024), ("v", 1024), ("sga", 2048), ("sgb", 2048)])[1], 3072
        cm = mx[:, a0:a0 + b0].rearrange("p (h n) -> p h n", n=384)
        G = mx[:, a0:a0 + 3072].rearrange("p (b n) -> p b n", b=3)
        a1 = a0 + 3584
        lg, pr, pt = (mx[:, a1 + 768 * j:a1 + 768 * (j + 1)].rearrange("p (b n) -> p b n", b=2) for j in range(3))
        vt = Bx["u"].rearrange("p (c n) -> p c n", c=2)
        s2 = carve(Bx["small"], [("A", 24), ("B", 24)] + [(k, 16) for k in
                   ("dt", "re", "im", "ta", "r", "em", "den", "ph", "sh", "sn", "l2", "kr", "ki", "t1", "t2", "f", "ab",
                    "ln", "lf", "mxn", "sum", "rec", "cs")], 500)

        (s_mod_used, s_hi_ready, s_lo_ready, s_unit_done, s_bank0, s_bank1) = (sem(n) for n in """mod_used hi_ready lo_ready unit_done bank0 bank1""".split())
        (s_pe_stat, s_sq_done, s_sqrt_done, s_hf_done, s_hhi_done, s_hlo_done, s_gate_th, s_hid_done,
         s_ghi_done, s_glo_done, s_x_done, s_y_copied, s_mod_sb, s_c_th, s_csil_done, s_dve_self,
         s_act_self, s_pe_ba, s_ba_ap, s_act_ap, s_gates_done, s_pe_gc, s_gc_sb, s_dd_done, s_act_eg,
         s_pe_grow, s_dpre, s_egr_done, s_dec_done, s_decm_done, s_pool_db, s_pe_brow, s_lt_half,
         s_conv_done, s_th_done, s_silu_done, s_qk_sqrt, s_qk_ready, s_pe_kk, s_lt_done, s_qk_done,
         s_pe_tok, s_kd_done, s_vb_done, s_xt_done, s_pool_lts, s_pe_x0, s_x0_sb, s_pe_t, s_t_sb, s_pe_dx,
         s_x_upd, s_z_th, s_c_done, s_pe_u0, s_vn0_done, s_pe_s, s_s_done, s_pe_w, s_w_done, s_pe_u1,
         s_vn1_done, s_qdec_done, s_pe_o, s_os_sqrt, s_ab_done, s_co_dve, s_co_act, s_cre_done, s_tab_arg,
         s_tab_frac, s_tab_sin, s_pe_bu, s_bu_sb, s_z_in, s_wv_done, s_s_sum, s_pe_y, s_g_in, s_g_tanh,
         s_pe_f, s_f_dve, s_f_act, s_lf_done, s_pe_ck, s_cm_done, s_pe_vt, s_vt_sb, s_pe_sc, s_lg_done,
         s_nm_done, s_p_exp, s_p_norm, s_pe_pt, s_pt_sb, s_pe_at, s_pads, s_dt_done) = (sem(n) for n in """pe_stat sq_done sqrt_done hf_done hhi_done hlo_done gate_th hid_done ghi_done glo_done
            x_done y_copied mod_sb c_th csil_done dve_self act_self pe_ba ba_ap act_ap gates_done
            pe_gc gc_sb dd_done act_eg pe_grow dpre egr_done dec_done decm_done pool_db pe_brow
            lt_half conv_done th_done silu_done qk_sqrt qk_ready pe_kk lt_done qk_done pe_tok
            kd_done vb_done xt_done pool_lts pe_x0 x0_sb pe_t t_sb pe_dx x_upd z_th c_done pe_u0
            vn0_done pe_s s_done pe_w w_done pe_u1 vn1_done qdec_done pe_o os_sqrt ab_done co_dve
            co_act cre_done tab_arg tab_frac tab_sin pe_bu bu_sb z_in wv_done s_sum pe_y g_in g_tanh
            pe_f f_dve f_act lf_done pe_ck cm_done pe_vt vt_sb pe_sc lg_done nm_done p_exp p_norm
            pe_pt pt_sb pe_at pads dt_done""".split())
        banks = [s_bank0, s_bank1]
        loaded = [sem(f"loaded{i}") for i in range(RAWS)]
        con_in, x_ld, p1_ld, p2_ld, stored = (sem(n) for n in ("con_in", "x_ld", "p1_ld", "p2_ld", "stored"))

        chunks = []
        for B, L, kind, i, n in NUMBERED:
            if kind == "mod":
                chunks.append(("mod", n["mod"] + 1))
            else:
                for v in range(n["split"], n["split"] + UNITS_OF.get(kind, 0)):
                    if v % 2 == 0:
                        chunks.append(("split", v + 2))
        chunk_of_unit = [c for c, (kind, _) in enumerate(chunks) if kind == "split" for _ in range(2)]
        chunk_of_mod = [c for c, (kind, _) in enumerate(chunks) if kind == "mod"]

        def evacuated(e, *step):
            p = AT[step]["pair"]
            e.wait_ge(banks[p % 2], p // 2 + 1)

        def arrived(e, chunk):
            e.wait_ge(loaded[chunk % RAWS], 16 * (chunk // RAWS + 1))

        block = ctx.enter_context(nc.Block())

        @block.sync
        def _(sp):
            sp.dma_start(con[:], const_in).then_inc(con_in, 16)
            sp.dma_start(x[:], x_in).then_inc(x_ld, 16)
            sp.dma_start(par1[:], p1_in).then_inc(p1_ld, 16)
            for c in range(len(chunks)):
                if c >= RAWS:
                    kind, n = chunks[c - RAWS]
                    if kind == "mod":
                        sp.wait_ge(s_mod_used, n)
                    else:
                        sp.wait_ge(s_lo_ready, n)
                sp.dma_start(raw[:, c % RAWS, :], w[c]).then_inc(loaded[c % RAWS], 16)
                if c == 6:
                    sp.dma_start(par2[:], p2_in).then_inc(p2_ld, 16)
            for j in range(4):
                sp.wait_ge(s_x_done, TOTAL["x"] - 8 + 2 * (j + 1))
                sp.dma_start(out[:, 2 * j:2 * j + 2, :], x[:, 2 * j:2 * j + 2, :]).then_inc(stored, 16)
            sp.wait_ge(stored, 16 * 4)

        @block.tensor
        def _(pe):
            mm, tr = nc.tensor.matmul, nc.tensor.transpose

            def product(unit, blocks, r_hi, r_lo):
                slot = unit % SLOTS
                pe.wait_ge(s_lo_ready, unit + 1)
                for b, (o, kt, first, end) in enumerate(blocks):
                    hi = w_hi[:, slot, b * P:(b + 1) * P]
                    lo = w_lo[:, slot, b * P:(b + 1) * P]
                    mm(o, hi, r_hi[:, kt, :], start=first, stop=False, skip_group_check=True)
                    mm(o, hi, r_lo[:, kt, :], start=False, stop=False, skip_group_check=True)
                    last = mm(o, lo, r_hi[:, kt, :], start=False, stop=end, skip_group_check=True)
                last.then_inc(s_unit_done, 1)

            def heads(c):
                return [(h, c * HEADS + h, slice(h * P, (h + 1) * P)) for h in range(HEADS)]

            def sum_squares(n):
                for j in range(4):
                    pe.wait_ge(s_sq_done, n + j + 1)
                    for e in range(2):
                        last = mm(stat[:, 0:T], ones, sq[:, j % 2, e * T:(e + 1) * T], start=(j == 0 and e == 0),
                                  stop=(j == 3 and e == 1))
                    last.then_inc(s_pe_stat, 1)

            pe.wait_ge(con_in, 16)
            pe.wait_ge(p1_ld, 16)
            for B, L, kind, i, n in NUMBERED:
                bank = stream[n["pair"] % 2]
                if kind in ("pair", "out", "mout", "gu"):
                    if n["pair"] // 2 > 0:
                        pe.wait_ge(banks[n["pair"] % 2], n["pair"] // 2)
                    if i == 0:
                        pe.wait_ge(s_hlo_done, n["h"])
                    for e in range(2):
                        product(n["split"] + e, [(bank[:, e, :], kt, kt == 0, kt == DT - 1) for kt in range(DT)],
                                h_hi, h_lo)
                elif kind in ("aout", "glu"):
                    pe.wait_ge(banks[n["pair"] % 2], n["pair"] // 2)
                    if kind == "aout":
                        pe.wait_ge(s_hlo_done, n["h"])
                    else:
                        pe.wait_ge(s_glo_done, AT[2, L, "gelu", 0]["g"] + 4)
                    product(n["split"], [(bank[:, m, :], kt, kt == 0, kt == 3) for m in range(2) for kt in range(4)],
                            h_hi if kind == "aout" else g_hi, h_lo if kind == "aout" else g_lo)
                elif kind == "down":
                    for e in range(2):
                        row = 2 * i + e
                        base = n["g"] - min(2 * i + 3, FT)
                        pe.wait_ge(s_glo_done, base + row + 1)
                        product(n["split"] + e,
                                [(work[m // 2][:, (m % 2) * T:(m % 2 + 1) * T], row % 4, row == 0 and m % 2 == 0,
                                  row == FT - 1) for m in range(DT)], g_hi, g_lo)
                elif kind == "mod":
                    chunk = chunk_of_mod[n["mod"]]
                    arrived(pe, chunk)
                    if i == 0:
                        pe.wait_ge(s_csil_done, 1)
                        if L > 0:
                            pe.wait_ge(s_mod_sb, L)
                    for e in range(2):
                        col = 2 * i + e
                        for kt in range(DT):
                            at = e * UNIT + kt * P
                            last = mm(modp[:, col:col + 1], raw[:, chunk % RAWS, at:at + P], csil[:, 1, kt:kt + 1],
                                      start=(kt == 0), stop=(kt == DT - 1))
                    last.then_inc(s_mod_used, 1)
                elif kind in ("norm", "pre", "post", "final"):
                    sum_squares(n["sq"])
                elif kind == "gates":
                    pe.wait_ge(s_hf_done, n["h"])
                    for c in range(TT):
                        for kt in range(DT):
                            last = mm(work[0][:, c * 8:c * 8 + 8], hf[:, kt, c * P:(c + 1) * P],
                                      p1_(L, "w_ba", kt * 8, kt * 8 + 8), start=(kt == 0), stop=(kt == DT - 1))
                    last.then_inc(s_pe_ba, 1)
                elif kind == "decay":
                    pe.wait_ge(s_gates_done, L + 1)
                    mm(work[1][:, 0:8], triu, sm["g"], start=True, stop=True)
                    mm(work[1][:, 8:16], ones, sm["g"], start=True, stop=True).then_inc(s_pe_gc, 1)
                    for c in range(TT):
                        for h, r, cols in heads(c):
                            last = mm(work[2 + c][:, cols], sm["g"][:, r:r + 1].to_broadcast([P, P]), triu,
                                      start=True, stop=True)
                        last.then_inc(s_pe_grow, 1)
                elif kind == "brow":
                    pe.wait_ge(s_pool_db, 8 * (L + 1))
                    pe.wait_ge(s_gc_sb, L + 1)
                    for c in range(TT):
                        for h, r, cols in heads(c):
                            last = mm(work[c][:, cols], ones, lts[:, r, :], start=True, stop=True)
                        last.then_inc(s_pe_brow, 1)
                elif kind == "qknorm":
                    pe.wait_ge(s_lt_half, 2 * (L + 1))
                    pe.wait_ge(s_dpre, 8 * (L + 1))
                    pe.wait_ge(s_egr_done, L + 1)
                    for j in range(4):
                        pe.wait_ge(s_sq_done, n["sq"] + j + 1)
                        mm(work[j][:], ones, sq[:, j % 2, :], start=True, stop=True).then_inc(s_pe_stat, 1)
                elif kind == "kk":
                    pe.wait_ge(s_qk_ready, 4 * (L + 1))
                    for c in range(TT):
                        for h, r, cols in heads(c):
                            kc = kT[:, h, c * P:(c + 1) * P]
                            mm(work[c][:, cols], kc, kc, start=True, stop=True)
                            last = mm(work[2 + c][:, cols], kc, qT[:, h, c * P:(c + 1) * P], start=True, stop=True)
                        last.then_inc(s_pe_kk, 1)
                elif kind == "tok":
                    pe.wait_ge(s_lt_done, 2 * (L + 1))
                    pe.wait_ge(s_qk_done, 2 * (L + 1))
                    pe.wait_ge(s_silu_done, 6 * (L + 1))
                    for c in range(TT):
                        for h, r, cols in heads(c):
                            tr(work[c][:, cols], kT[:, h, c * P:(c + 1) * P], ident)
                            last = tr(work[2 + c][:, cols], vT[:, h, c * P:(c + 1) * P], ident)
                        last.then_inc(s_pe_tok, 1)
                elif kind == "level" and i == 0:
                    pe.wait_ge(s_kd_done, 8 * (L + 1))
                    pe.wait_ge(s_vb_done, 8 * (L + 1))
                    for c in range(TT):
                        pe.wait_ge(s_xt_done, 2 * L + c + 1)
                        for h, r, cols in heads(c):
                            last = tr(work[2 * c][:, cols], xt[:, r, :], ident)
                        last.then_inc(s_pe_x0, 1)
                elif kind == "level":
                    for c in range(TT):
                        pe.wait_ge(s_pool_lts, 12 * L + 2 * (i - 1) + c + 1)
                        if i == 1:
                            pe.wait_ge(s_x0_sb, 2 * L + c + 1)
                        else:
                            pe.wait_ge(s_x_upd, 12 * L + 2 * (i - 2) + c + 1)
                        for h, r, cols in heads(c):
                            last = mm(work[2 * c][:, cols], lts[:, r, :], xi[:, r, :], start=True, stop=True)
                        last.then_inc(s_pe_t, 1)
                    for c in range(TT):
                        pe.wait_ge(s_t_sb, 12 * L + 2 * (i - 1) + c + 1)
                        for h, r, cols in heads(c):
                            if i < 6:
                                mm(work[2 * c][:, cols], xt[:, r, :], tt[:, r, :], start=True, stop=True)
                            last = mm(work[2 * c + 1][:, cols], tt[:, r, :], xt[:, r, :], start=True, stop=True)
                        last.then_inc(s_pe_dx, 1)
                elif kind == "scan":
                    pe.wait_ge(s_x_upd, 12 * (L + 1))
                    for h, r, cols in heads(0):
                        last = mm(work[0][:, cols], xt[:, h, :], vb[:, h, :], start=True, stop=True)
                    last.then_inc(s_pe_u0, 1)
                    for h, r, cols in heads(1):
                        last = mm(work[1][:, cols], kd[:, r, :], xt[:, r, :], start=True, stop=True)
                    last.then_inc(s_pe_w, 1)
                    pe.wait_ge(s_vn0_done, L + 1)
                    for h, r, cols in heads(0):
                        last = mm(work[2][:, cols], kd[:, h, :], vn0[:, h, :], start=True, stop=True)
                    last.then_inc(s_pe_s, 1)
                    pe.wait_ge(s_w_done, L + 1)
                    pe.wait_ge(s_s_done, L + 1)
                    for h, r, cols in heads(1):
                        mm(work[3][:, cols], xt[:, r, :], vb[:, r, :], start=True, stop=False)
                        last = mm(work[3][:, cols], w_sb[:, h, :], s_sb[:, h, :], start=False, stop=True)
                    last.then_inc(s_pe_u1, 1)
                    pe.wait_ge(s_vn1_done, L + 1)
                    pe.wait_ge(s_qdec_done, L + 1)
                    for h in range(HEADS):
                        o, a = work[h // 2], (h % 2) * T
                        mm(o[:, a:a + P], vn0[:, h, :], qk[:, h, :], start=True, stop=True)
                        mm(o[:, a + P:a + T], s_sb[:, h, :], qdec[:, h, :], start=True, stop=False)
                        last = mm(o[:, a + P:a + T], vn1[:, h, :], qk[:, 4 + h, :], start=False, stop=True)
                        if h % 2:
                            last.then_inc(s_pe_o, 1)
                elif kind == "headnorm":
                    for j, dst in enumerate((work[2], work[3], stat, work[2])):
                        pe.wait_ge(s_sq_done, n["sq"] + j + 1)
                        if j == 3:
                            pe.wait_ge(s_os_sqrt, 4 * L + 1)
                        mm(dst[:], ones, sq[:, j % 2, :], start=True, stop=True).then_inc(s_pe_stat, 1)
                elif kind == "forget":
                    pe.wait_ge(s_g_in, 4 * (L + 1))
                    pe.wait_ge(s_bu_sb, ST * (L + 1))
                    for c in range(TT):
                        for kt in range(DT):
                            last = mm(work[0][:, c * 8:c * 8 + 8], hf[:, kt, c * P:(c + 1) * P],
                                      p2_(L, "w_f", kt * 8, kt * 8 + 8), start=(kt == 0), stop=(kt == DT - 1))
                    last.then_inc(s_pe_f, 1)
                    pe.wait_ge(s_lf_done, L + 1)
                    for j in range(AH // 2):
                        for e in range(2):
                            h = 2 * j + e
                            mm(work[j][:, e * T:(e + 1) * T], s2["lf"][:, h:h + 1].to_broadcast([P, P]), triu_ones,
                               start=True, stop=False, skip_group_check=True)
                            last = mm(work[j][:, e * T + P:(e + 1) * T], s2["lf"][:, 8 + h:9 + h].to_broadcast([P, P]),
                                      triu, start=False, stop=True, skip_group_check=True)
                        last.then_inc(s_pe_ck, 1)
                elif kind == "ssm":
                    if i == 0:
                        evacuated(pe, 2, L, "pair", 0)
                        evacuated(pe, 2, L, "pair", 1)
                        pe.wait_ge(s_cre_done, L + 1)
                    if ST * L + i - 1 > 0:
                        pe.wait_ge(s_bu_sb, ST * L + i - 1)
                    ut, q = i // 4, i % 4
                    rows = slice(32 * q, 32 * q + 32)
                    for e, name in enumerate(("b_re", "b_im")):
                        last = mm(work[i % 2][:, e * T:(e + 1) * T], p2_(L, name, ut * P, ut * P + P)[rows, :],
                                  u2[rows, ut, :], start=True, stop=True)
                    last.then_inc(s_pe_bu, 1)
                    for k in ([i - 2] if i >= 2 else []) + ([i - 1, i] if i == ST - 1 else []):
                        pe.wait_ge(s_s_sum, 2 * (ST * L + k + 1))
                        kt, kq = k // 4, k % 4
                        o = work[2 + kt // 2][32 * kq:32 * kq + 32, (kt % 2) * T:(kt % 2 + 1) * T]
                        mm(o, cp[:, 0, k, :], sst[:, k % 2, 0:T], start=True, stop=False, skip_group_check=True)
                        mm(o, cp[:, 1, k, :], sst[:, k % 2, T:2 * T], start=False, stop=True,
                           skip_group_check=True).then_inc(s_pe_y, 1)
                elif kind == "vtok":
                    pe.wait_ge(s_cm_done, 8 * (L + 1))
                    for c in range(TT):
                        for hp in range(4):
                            last = tr(work[c][:, hp * P:(hp + 1) * P], v2[:, hp, c * P:(c + 1) * P], ident)
                        last.then_inc(s_pe_vt, 1)
                elif kind == "head":
                    hp, e = i // 2, i % 2
                    rows = slice(64 * e, 64 * e + 64)
                    if i == 0:
                        pe.wait_ge(s_vt_sb, 2 * (L + 1))
                    if AH * L + i - 1 > 0:
                        pe.wait_ge(s_lg_done, AH * L + i - 1)
                    mm(work[i % 2][:, 0:T], q2[rows, hp, P:T], k2[rows, hp, :], start=True, stop=True)
                    mm(work[i % 2][:, T:T + P], q2[rows, hp, 0:P], k2[rows, hp, 0:P], start=True,
                       stop=True).then_inc(s_pe_sc, 1)
                    for k in ([i - 1] if i >= 1 else []) + ([i] if i == AH - 1 else []):
                        kp, ke = k // 2, k % 2
                        pe.wait_ge(s_p_norm, 2 * (AH * L + k + 1))
                        if AH * L + k > 0:
                            pe.wait_ge(s_pt_sb, AH * L + k)
                        tr(modp[:, 0:P], pr[:, k % 2, T:T + P], ident)
                        tr(modp[:, P:T], pr[:, k % 2, 0:P], ident)
                        tr(modp[:, T:T + P], pr[:, k % 2, P:T], ident).then_inc(s_pe_pt, 1)
                        pe.wait_ge(s_pt_sb, AH * L + k + 1)
                        if kp >= 2:
                            pe.wait_ge(s_hf_done, n["h"] + kp - 1)
                        o = work[2 + kp % 2]
                        orow = slice(64 * ke, 64 * ke + 64)
                        mm(o[orow, 0:T], vt[:, 0, k * AD:(k + 1) * AD], pt[:, k % 2, 0:T], start=True, stop=False,
                           skip_group_check=True)
                        mm(o[orow, P:T], vt[:, 1, k * AD:(k + 1) * AD], pt[:, k % 2, T:T + P], start=False, stop=True,
                           skip_group_check=True).then_inc(s_pe_at, 1)

        @block.scalar
        def _(act):
            f = nc.scalar.activation
            links = [0]

            def link(ins):
                links[0] += 1
                ins.then_inc(s_act_self, 1)
                act.wait_ge(s_act_self, links[0])

            fed = [0]

            def round_weights(limit):
                while fed[0] < min(limit, TOTAL["split"]):
                    v = fed[0]
                    if v % 2 == 0:
                        arrived(act, chunk_of_unit[v])
                    if v - SLOTS + 1 > 0:
                        act.wait_ge(s_unit_done, v - SLOTS + 1)
                    f(w_hi[:, v % SLOTS, :], raw[:, chunk_of_unit[v] % RAWS, (v % 2) * UNIT:(v % 2 + 1) * UNIT],
                      ACT.Copy).then_inc(s_hi_ready, 1)
                    fed[0] += 1

            def squares(n, sources, waits):
                for j in range(4):
                    waits(j)
                    if n + j - 1 > 0:
                        act.wait_ge(s_pe_stat, n + j - 1)
                    f(sq[:, j % 2, :], sources(j), ACT.Square).then_inc(s_sq_done, 1)

            def round_h(n, t, first=0):
                act.wait_ge(s_hf_done, n["h"] + t - first + 1)
                f(h_hi[:, t, :], hf[:, t, :], ACT.Copy).then_inc(s_hhi_done, 1)

            def round_g(g, slot):
                act.wait_ge(s_hid_done, g + 1)
                f(g_hi[:, slot, :], hid[:, g % 2, :], ACT.Copy).then_inc(s_ghi_done, 1)

            def root(n):
                act.wait_ge(s_pe_stat, n["sq"] + 4)
                f(std[:], stat[:, 0:T], ACT.Sqrt, bias=EPS, scale=1.0 / D).then_inc(s_sqrt_done, 1)

            act.wait_ge(con_in, 16)
            f(csil[:, 0, :], c_("c"), ACT.Tanh, scale=0.5).then_inc(s_c_th, 1)
            act.wait_ge(x_ld, 16)
            act.wait_ge(p1_ld, 16)
            for B, L, kind, i, n in NUMBERED:
                bank = stream[n["pair"] % 2]
                units = UNITS_OF.get(kind, 0)
                free = banks[n["pair"] % 2]
                if units:
                    round_weights(n["split"] + units + 2)
                    if kind != "down":
                        act.wait_ge(s_unit_done, n["split"] + units)
                if kind in ("norm", "pre", "post", "final"):
                    if kind == "norm" and i == 1:
                        squares(n["sq"], lambda j: x[:, 2 * j:2 * j + 2, :], lambda j: evacuated(act, 1, L, "out", j))
                    elif kind == "post" and i == 1:
                        squares(n["sq"], lambda j: hf[:, 2 * j:2 * j + 2, :], lambda j: evacuated(act, 2, L, "mout", j))
                    elif kind == "post":
                        squares(n["sq"], lambda j: hf[:, 2 * j:2 * j + 2, :],
                                lambda j: act.wait_ge(s_y_copied, n["y"] + j + 1))
                    else:
                        base = n["x"] - 4 * B

                        def x_ready(j):
                            if base >= 0:
                                act.wait_ge(s_x_done, base + B * (j + 1))
                        squares(n["sq"], lambda j: x[:, 2 * j:2 * j + 2, :], x_ready)
                    root(n)
                    if kind in ("norm", "pre"):
                        if n["split"] > 0:
                            act.wait_ge(s_unit_done, n["split"])
                        for t in range(DT):
                            round_h(n, t)
                elif kind == "gates":
                    act.wait_ge(s_ba_ap, L + 1)
                    b_part = sm["ba"].rearrange("p (c n) -> p c n", c=2)[:, :, 0:4]
                    f(sm["tb"].rearrange("p (c n) -> p c n", c=2), b_part, ACT.Tanh, scale=0.5)
                    f(sm["ea"], p1_(L, "a_log"), ACT.Exp)
                    link(f(sm["ab"], sm["ap"], ACT.Abs))
                    link(f(sm["ab"], sm["ab"], ACT.Exp, scale=-1.0))
                    f(sm["ln"], sm["ab"], ACT.Ln, bias=1.0).then_inc(s_act_ap, 1)
                elif kind == "decay":
                    act.wait_ge(s_dd_done, L + 1)
                    f(sm["eg"], sm["gc"][:, 0:8], ACT.Exp)
                    f(sm["ekd"], sm["d"], ACT.Exp).then_inc(s_act_eg, 1)
                    act.wait_ge(s_pe_grow, 2 * (L + 1))
                    f(egr, work[3][:], ACT.Exp).then_inc(s_egr_done, 1)
                    for c in range(TT):
                        act.wait_ge(s_dpre, 8 * L + 4 * c + 4)
                        f(dec[:, 4 * c:4 * c + 4, :], dec[:, 4 * c:4 * c + 4, :], ACT.Exp).then_inc(s_dec_done, 1)
                elif kind == "pair" and B == 1 and i < 6:
                    if i >= 2:
                        act.wait_ge(s_conv_done, 12 * L + 2 * (i - 1))
                    elif L == 0:
                        act.wait_ge(s_pads, 1)
                    f(rawp[:, i % 2, :, 3:3 + T], bank[:], ACT.Copy).then_inc(free, 1)
                    act.wait_ge(s_conv_done, 12 * L + 2 * (i + 1))
                    if 6 * L + i - 1 > 0:
                        act.wait_ge(s_silu_done, 6 * L + i - 1)
                    f(th[:, 2 * (i % 2):2 * (i % 2) + 2, :], yv[:, 2 * (i % 2):2 * (i % 2) + 2, :], ACT.Tanh,
                      scale=0.5).then_inc(s_th_done, 1)
                elif kind == "pair" and B == 1 and i < 8:
                    f(zs[:, 2 * (i - 6):2 * (i - 6) + 2, :], bank[:], ACT.Tanh, scale=0.5).then_inc(s_z_th, 1)
                elif kind == "pair" and B == 1 and i < 12:
                    act.wait_ge(s_silu_done, 6 * (L + 1))
                    f(th[:, i - 8, :], bank[:, 0, :], ACT.Copy).then_inc(s_c_done, 1)
                elif kind == "qknorm":
                    src = [qT[:, 0:2, :], qT[:, 2:4, :], kT[:, 0:2, :], kT[:, 2:4, :]]
                    squares(n["sq"], lambda j: src[j], lambda j: act.wait_ge(s_silu_done, 6 * L + j + 1))
                    for j in range(4):
                        act.wait_ge(s_pe_stat, n["sq"] + j + 1)
                        scale = float(HD) if j < 2 else 1.0
                        f(sd[j], work[j][:], ACT.Sqrt, scale=scale, bias=4 * EPS * scale).then_inc(s_qk_sqrt, 1)
                elif kind == "tok":
                    for c in range(TT):
                        act.wait_ge(s_pe_tok, 2 * L + c + 1)
                        for h in range(HEADS):
                            r = c * HEADS + h
                            by = sm["ekd"] if c == 0 else sm["bke"]
                            f(kd[:, r, :], work[c][:, h * P:(h + 1) * P], ACT.Copy, scale=by[:, r:r + 1])\
                                .then_inc(s_kd_done, 1)
                elif kind == "level":
                    for c in range(TT):
                        if i == 0:
                            act.wait_ge(s_qdec_done, L + 1)
                            act.wait_ge(s_pe_x0, 2 * L + c + 1)
                            f(xi[:, 4 * c:4 * c + 4, :], work[2 * c][:], ACT.Copy).then_inc(s_x0_sb, 1)
                        else:
                            act.wait_ge(s_pe_t, 12 * L + 2 * (i - 1) + c + 1)
                            f(tt[:, 4 * c:4 * c + 4, :], work[2 * c][:], ACT.Copy).then_inc(s_t_sb, 1)
                elif kind == "scan":
                    for src, got, dst, k, done in ((0, s_pe_u0, vn0, 1.0, s_vn0_done), (1, s_pe_w, w_sb, -1.0, s_w_done),
                                                   (2, s_pe_s, s_sb, 1.0, s_s_done), (3, s_pe_u1, vn1, 1.0, s_vn1_done)):
                        act.wait_ge(got, L + 1)
                        f(dst, work[src][:], ACT.Copy, scale=k).then_inc(done, 1)
                elif kind == "headnorm":
                    src = [work[0][:], work[1][:], sc[:, 0:2, :], sc[:, 2:4, :]]

                    def ready(j):
                        if j < 2:
                            act.wait_ge(s_pe_o, 2 * L + j + 1)
                        else:
                            evacuated(act, 1, L, "pair", 10 + j)
                    squares(n["sq"], lambda j: src[j], ready)
                    for j, b in enumerate((work[2], work[3], stat, work[2])):
                        act.wait_ge(s_pe_stat, n["sq"] + j + 1)
                        k = 4.0 if j < 2 else 1.0
                        f(sd[j], b[:], ACT.Sqrt, scale=k / HD, bias=k * EPS).then_inc(s_os_sqrt, 1)
                    act.wait_ge(s_unit_done, n["split"])
                    for t in range(DT):
                        round_h(n, t)
                elif kind == "gu":
                    if n["g"] - 1 > 0:
                        act.wait_ge(s_hid_done, n["g"] - 1)
                    f(gate_t[:, n["g"] % 2, :], bank[:, 0, :], ACT.Tanh, scale=0.5).then_inc(s_gate_th, 1)
                    round_g(n["g"], i % 4)
                elif kind == "coef":
                    t = s2
                    act.wait_ge(p2_ld, 16)
                    f(t["dt"], p2_(L, "log_dt"), ACT.Exp).then_inc(s_dt_done, 1)
                    act.wait_ge(s_co_dve, 2 * L + 1)
                    f(t["ta"], t["re"], ACT.Tanh, scale=0.5)
                    act.wait_ge(s_co_dve, 2 * L + 2)
                    f(t["sh"], t["ph"], ACT.Sin, scale=3.1415925)
                    f(t["sn"], t["ph"], ACT.Sin, scale=6.2831850).then_inc(s_co_act, 1)
                elif kind == "pair" and B == 2 and i < 8:
                    dst = (u2, q2, k2, v2)[i // 2]
                    f(dst[:, 2 * (i % 2):2 * (i % 2) + 2, :], bank[:], ACT.Copy).then_inc(free, 1)
                elif kind == "pair" and B == 2:
                    dst, t = (sga, i - 8) if i < 12 else (sgb, i - 12)
                    f(dst[:, 2 * t:2 * t + 2, :], bank[:], ACT.Tanh, scale=0.5).then_inc(free, 1)
                elif kind == "ssm":
                    act.wait_ge(s_tab_frac, ST * L + i + 1)
                    if 2 * (ST * L + i - 1) > 0:
                        act.wait_ge(s_s_sum, 2 * (ST * L + i - 1))
                    f(tab[:, i % 2, 0:512], Bx["arg"], ACT.Sin, scale=6.2831850)
                    f(tab[:, i % 2, 512:768], Bx["arg"][:, 0:256], ACT.Sin, scale=6.2831850).then_inc(s_tab_sin, 1)
                    act.wait_ge(s_pe_bu, ST * L + i + 1)
                    if 2 * (ST * L + i - 1) > 0:
                        act.wait_ge(s_z_in, 2 * (ST * L + i - 1))
                    f(bu[:, i % 2, :], work[i % 2][:], ACT.Copy).then_inc(s_bu_sb, 1)
                elif kind == "gelu":
                    act.wait_ge(s_g_in, 4 * (L + 1))
                    f(G[:, 1, :], G[:, 1, :], ACT.Tanh, scale=0.7978845608028654).then_inc(s_g_tanh, 1)
                    for t in range(4):
                        round_g(n["g"] + t, t)
                elif kind == "forget":
                    act.wait_ge(s_f_dve, L + 1)
                    link(f(s2["ab"], s2["f"], ACT.Abs))
                    link(f(s2["ab"], s2["ab"], ACT.Exp, scale=-1.0))
                    f(s2["ln"], s2["ab"], ACT.Ln, bias=1.0).then_inc(s_f_act, 1)
                elif kind == "vtok":
                    for c in range(TT):
                        act.wait_ge(s_pe_vt, 2 * L + c + 1)
                        f(vt[:, c, :], work[c][:], ACT.Copy).then_inc(s_vt_sb, 1)
                elif kind == "head":
                    if AH * L + i - 1 > 0:
                        act.wait_ge(s_pe_pt, AH * L + i - 1)
                    for e, cols in enumerate((slice(0, T), slice(T, T + P))):
                        k = 2 * i + e
                        act.wait_ge(s_nm_done, 2 * AH * L + k + 1)
                        f(pr[:, i % 2, cols], lg[:, i % 2, cols], ACT.Exp, bias=s2["mxn"][:, k:k + 1],
                          accum_out=s2["sum"][:, k:k + 1]).then_inc(s_p_exp, 1)
                    for k in ([i - 1] if i >= 1 else []) + ([i] if i == AH - 1 else []):
                        act.wait_ge(s_pe_pt, AH * L + k + 1)
                        if AH * L + k - 1 > 0:
                            act.wait_ge(s_pe_at, AH * L + k - 1)
                        f(pt[:, k % 2, :], modp[:, 0:384], ACT.Copy).then_inc(s_pt_sb, 1)
                    if i == AH - 1:
                        act.wait_ge(s_unit_done, n["split"])
                        for t in range(4):
                            round_h(n, t)
                elif kind == "glu":
                    act.wait_ge(s_hf_done, n["h"] - 1)
                    f(gate_t[:, i % 2, :], bank[:, 1, :], ACT.Tanh, scale=0.5).then_inc(s_gate_th, 1)
                    round_h(n, i, first=i)

        @block.vector
        def _(dve):
            v = nc.vector
            links = [0]

            def link(ins):
                links[0] += 1
                ins.then_inc(s_dve_self, 1)
                dve.wait_ge(s_dve_self, links[0])

            fed = [0]

            def low_weights(limit):
                while fed[0] < min(limit, TOTAL["split"]):
                    q = fed[0]
                    dve.wait_ge(s_hi_ready, q + 1)
                    v.tensor_tensor(w_lo[:, q % SLOTS, :],
                                    raw[:, chunk_of_unit[q] % RAWS, (q % 2) * UNIT:(q % 2 + 1) * UNIT],
                                    w_hi[:, q % SLOTS, :].bitcast(F32), ALU.subtract).then_inc(s_lo_ready, 1)
                    fed[0] += 1

            def low_h(n, t, first=0):
                dve.wait_ge(s_hhi_done, n["h"] + t - first + 1)
                v.tensor_tensor(h_lo[:, t, :], hf[:, t, :], h_hi[:, t, :].bitcast(F32), ALU.subtract)\
                    .then_inc(s_hlo_done, 1)

            def inverse_root():
                link(v.reciprocal(rstd[:], std[:]))

            def turns(i, k):
                if k > 0:
                    dve.wait_ge(s_tab_sin, k)
                for e in range(2):
                    ins = v.tensor_scalar(Bx["arg"][:, e * T:(e + 1) * T], c_("time"), s2["ph"][:, i:i + 1], 0.25 * e,
                                          ALU.mult, ALU.add)
                link(ins)
                v.tensor_scalar(Bx["rnd"], Bx["arg"], ROUND, ROUND, ALU.add, ALU.subtract).then_inc(s_tab_arg, 1)

            link(v.memset(rawp[:, :, :, 0:3], 0.0))
            v.memset(scp[:, :, 0:2], 0.0).then_inc(s_pads, 1)
            dve.wait_ge(s_c_th, 1)
            dve.wait_ge(con_in, 16)
            link(v.scalar_tensor_tensor(csil[:, 0, :], csil[:, 0, :], 1.0, c_("c"), ALU.add, ALU.mult))
            v.tensor_scalar(csil[:, 1, :], csil[:, 0, :], 0.5, None, ALU.mult).then_inc(s_csil_done, 1)
            dve.wait_ge(x_ld, 16)
            dve.wait_ge(p1_ld, 16)
            for B, L, kind, i, n in NUMBERED:
                bank = stream[n["pair"] % 2]
                units = UNITS_OF.get(kind, 0)
                free = banks[n["pair"] % 2]
                if units:
                    low_weights(n["split"] + units + 2)
                    if kind != "down":
                        dve.wait_ge(s_unit_done, n["split"] + units)
                if kind in ("norm", "pre"):
                    dve.wait_ge(s_sqrt_done, n["norm"] + 1)
                    inverse_root()
                    gain = p1_(L, f"norm{i + 1}") if B == 1 else s2["A"][:, 8 * i:8 * i + 8]
                    for t in range(DT):
                        ins = v.scalar_tensor_tensor(hf[:, t, :], x[:, t, :], gain[:, t:t + 1], rstd[:], ALU.mult,
                                                     ALU.mult)
                        if B == 2:
                            link(ins)
                            ins = v.tensor_scalar(hf[:, t, :], hf[:, t, :], modv[:, L, i, 0, t:t + 1], None, ALU.add)
                        ins.then_inc(s_hf_done, 1)
                        if t:
                            low_h(n, t - 1)
                    low_h(n, DT - 1)
                elif kind == "final":
                    dve.wait_ge(s_sqrt_done, n["norm"] + 1)
                    inverse_root()
                    for t in range(DT):
                        v.scalar_tensor_tensor(x[:, t, :], x[:, t, :], c_("final", t, t + 1), rstd[:], ALU.mult, ALU.mult)\
                            .then_inc(s_x_done, 1)
                elif kind == "post":
                    if i != 1:
                        dve.wait_ge(s_unit_done, n["split"])
                        for j in range(4):
                            v.tensor_copy(hf[:, 2 * j:2 * j + 2, :], work[j][:]).then_inc(s_y_copied, 1)
                    dve.wait_ge(s_sqrt_done, n["norm"] + 1)
                    inverse_root()
                    for t in range(DT):
                        link(v.scalar_tensor_tensor(hf[:, t, :], hf[:, t, :], s2["B"][:, 8 * i + t:8 * i + t + 1],
                                                    rstd[:], ALU.mult, ALU.mult))
                        v.tensor_tensor(x[:, t, :], x[:, t, :], hf[:, t, :], ALU.add).then_inc(s_x_done, 1)
                elif kind == "acc":
                    dve.wait_ge(s_unit_done, n["split"])
                    for j in range(4):
                        v.tensor_tensor(x[:, 2 * j:2 * j + 2, :], x[:, 2 * j:2 * j + 2, :],
                                        work[j][:].rearrange("p (n t) -> p n t", t=T), ALU.add).then_inc(s_x_done, 1)
                    dve.wait_ge(s_mod_used, n["mod"])
                    v.tensor_tensor(modv[:, L].rearrange("p a b c -> p (a b c)"), modp[:, 0:MODT], p1_(L, "mod_b"),
                                    ALU.add).then_inc(s_mod_sb, 1)
                elif kind == "gates":
                    dve.wait_ge(s_pe_ba, L + 1)
                    link(v.tensor_copy(sm["ba"], work[0][:, 0:16]))
                    ba = sm["ba"].rearrange("p (c n) -> p c n", c=2)
                    v.tensor_tensor(sm["ap"].rearrange("p (c n) -> p c n", c=2), ba[:, :, 4:8],
                                    p1_(L, "dt_bias").unsqueeze(1).to_broadcast([P, 2, 4]), ALU.add)\
                        .then_inc(s_ba_ap, 1)
                    dve.wait_ge(s_act_ap, L + 1)
                    v.tensor_scalar(sm["beta"], sm["tb"], 0.5, 0.5, ALU.mult, ALU.add)
                    v.tensor_scalar(sm["hb"], sm["tb"], 0.25, 0.25, ALU.mult, ALU.add)
                    link(v.scalar_tensor_tensor(sm["sp"], sm["ap"], 0.0, sm["ln"], ALU.max, ALU.add))
                    v.scalar_tensor_tensor(sm["g"].rearrange("p (c n) -> p c n", c=2),
                                           sm["sp"].rearrange("p (c n) -> p c n", c=2), -1.0,
                                           sm["ea"].unsqueeze(1).to_broadcast([P, 2, 4]), ALU.mult, ALU.mult)\
                        .then_inc(s_gates_done, 1)
                elif kind == "decay":
                    dve.wait_ge(s_pe_gc, L + 1)
                    v.tensor_copy(sm["gc"], work[1][:, 0:16]).then_inc(s_gc_sb, 1)
                    dve.wait_ge(s_gc_sb, L + 1)
                    v.tensor_tensor(sm["d"], sm["gc"][:, 8:16], sm["gc"][:, 0:8], ALU.subtract).then_inc(s_dd_done, 1)
                    for c in range(TT):
                        dve.wait_ge(s_pe_grow, 2 * L + c + 1)
                        if c == 1:
                            dve.wait_ge(s_egr_done, L + 1)
                        for h in range(HEADS):
                            r = c * HEADS + h
                            v.tensor_scalar(dec[:, r, :], work[2 + c][:, h * P:(h + 1) * P], sm["gc"][:, r:r + 1], 0.0,
                                            ALU.subtract, ALU.min).then_inc(s_dpre, 1)
                    dve.wait_ge(s_act_eg, L + 1)
                    link(v.tensor_tensor(sm["bke"], sm["beta"], sm["eg"], ALU.mult))
                elif kind == "brow":
                    for c in range(TT):
                        dve.wait_ge(s_decm_done, 2 * L + c + 1)
                        dve.wait_ge(s_pe_brow, 2 * L + c + 1)
                        v.tensor_tensor(A["lt"][:, 512 * c:512 * c + 512], A["dec"][:, 512 * c:512 * c + 512], work[c][:],
                                        ALU.mult).then_inc(s_lt_half, 1)
                elif kind == "pair" and B == 1 and i < 6:
                    evacuated(dve, B, L, kind, i)
                    if L == 0 and i == 0:
                        dve.wait_ge(s_pads, 1)
                    for k in range(TAPS):
                        for e in range(2):
                            tile = 2 * i + e
                            y = yv[:, 2 * (i % 2) + e, :]
                            src = rawp[:, i % 2, e, k:k + T]
                            tap = p1_(L, "conv", tile * TAPS + k, tile * TAPS + k + 1)
                            if k == 0:
                                ins = v.tensor_scalar(y, src, tap, None, ALU.mult)
                            else:
                                ins = v.scalar_tensor_tensor(y, src, tap, y, ALU.mult, ALU.add)
                            if k == TAPS - 1:
                                ins.then_inc(s_conv_done, 1)
                            elif e == 1:
                                link(ins)
                    dve.wait_ge(s_th_done, 6 * L + i + 1)
                    dst = (qT, kT, vT)[i // 2]
                    v.scalar_tensor_tensor(dst[:, 2 * (i % 2):2 * (i % 2) + 2, :], th[:, 2 * (i % 2):2 * (i % 2) + 2, :],
                                           1.0, yv[:, 2 * (i % 2):2 * (i % 2) + 2, :], ALU.add, ALU.mult)\
                        .then_inc(s_silu_done, 1)
                elif kind == "pair" and B == 1 and i < 8:
                    t = 2 * (i - 6)
                    dve.wait_ge(s_z_th, 2 * L + i - 5)
                    v.scalar_tensor_tensor(zs[:, t:t + 2, :], zs[:, t:t + 2, :], 1.0, bank[:], ALU.add, ALU.mult)\
                        .then_inc(free, 1)
                elif kind == "pair" and B == 1 and i < 12:
                    t = i - 8
                    dve.wait_ge(s_c_done, 4 * L + t + 1)
                    v.tensor_tensor(scp[:, t, 2:2 + T], th[:, t, :], bank[:, 1, :], ALU.mult).then_inc(free, 1)
                    evacuated(dve, B, L, kind, i)
                    for k in range(STAPS):
                        tap = p1_(L, "sconv", t * STAPS + k, t * STAPS + k + 1)
                        src = scp[:, t, k:k + T]
                        if k == 0:
                            link(v.tensor_scalar(sc[:, t, :], src, tap, None, ALU.mult))
                        else:
                            link(v.scalar_tensor_tensor(sc[:, t, :], src, tap, sc[:, t, :], ALU.mult, ALU.add))
                elif kind == "pair" and B == 1:
                    t = 2 * (i - 12)
                    v.tensor_tensor(sc[:, t:t + 2, :], sc[:, t:t + 2, :], bank[:], ALU.mult).then_inc(free, 1)
                elif kind == "qknorm":
                    for j in range(4):
                        dve.wait_ge(s_qk_sqrt, 4 * L + j + 1)
                        link(v.reciprocal(sd[j], sd[j]))
                        dst = (qT, kT)[j // 2][:, 2 * (j % 2):2 * (j % 2) + 2, :]
                        v.tensor_tensor(dst, dst, sd[j].rearrange("p (n t) -> p n t", t=T), ALU.mult)\
                            .then_inc(s_qk_ready, 1)
                elif kind == "kk":
                    for c in range(TT):
                        dve.wait_ge(s_pe_kk, 2 * L + c + 1)
                        dve.wait_ge(s_lt_half, 2 * L + c + 1)
                        half = slice(512 * c, 512 * c + 512)
                        four = slice(4 * c, 4 * c + 4)
                        v.tensor_tensor(A["lt"][:, half], A["lt"][:, half], work[c][:], ALU.mult)\
                            .then_inc(s_lt_done, 1)
                        v.tensor_tensor(A["qk"][:, half], A["dec"][:, half], work[2 + c][:], ALU.mult)\
                            .then_inc(s_qk_done, 1)
                        dve.wait_ge(s_lt_done, 2 * L + c + 1)
                        link(v.tensor_tensor(xt[:, four, :], lt[:, four, :],
                                             c_("m", 0, P).unsqueeze(1).to_broadcast([P, 4, P]), ALU.mult))
                        v.scalar_tensor_tensor(xt[:, four, :], xt[:, four, :], -1.0,
                                               ident.unsqueeze(1).to_broadcast([P, 4, P]), ALU.mult, ALU.add)\
                            .then_inc(s_xt_done, 1)
                elif kind == "tok":
                    for c in range(TT):
                        dve.wait_ge(s_pe_tok, 2 * L + c + 1)
                        for h in range(HEADS):
                            r = c * HEADS + h
                            v.tensor_scalar(vb[:, r, :], work[2 + c][:, h * P:(h + 1) * P], sm["hb"][:, r:r + 1], None,
                                            ALU.mult).then_inc(s_vb_done, 1)
                elif kind == "level" and i:
                    for c in range(TT):
                        dve.wait_ge(s_pe_dx, 12 * L + 2 * (i - 1) + c + 1)
                        half = slice(512 * c, 512 * c + 512)
                        if i < 6:
                            v.tensor_tensor(A["x"][:, half], A["x"][:, half], work[2 * c][:], ALU.subtract)
                        v.tensor_tensor(A["xt"][:, half], A["xt"][:, half], work[2 * c + 1][:], ALU.subtract)\
                            .then_inc(s_x_upd, 1)
                elif kind == "headnorm":
                    for j in range(4):
                        dve.wait_ge(s_os_sqrt, 4 * L + j + 1)
                        link(v.reciprocal(sd[j], sd[j]))
                        if j < 2:
                            two = hf[:, 2 * j:2 * j + 2, :]
                            link(v.scalar_tensor_tensor(two.rearrange("p n t -> p (n t)"), work[j][:],
                                                        p1_(L, "dn_g"), sd[j], ALU.mult, ALU.mult))
                            v.tensor_tensor(two, two, zs[:, 2 * j:2 * j + 2, :], ALU.mult).then_inc(s_hf_done, 2)
                        else:
                            for e in range(2):
                                t = 2 * (j - 2) + e
                                v.scalar_tensor_tensor(hf[:, 4 + t, :], sc[:, t, :], p1_(L, "sc_g", t, t + 1),
                                                       sd[j][:, e * T:(e + 1) * T], ALU.mult, ALU.mult)\
                                    .then_inc(s_hf_done, 1)
                    for t in range(DT):
                        low_h(n, t)
                elif kind == "out":
                    v.tensor_tensor(x[:, 2 * i:2 * i + 2, :], x[:, 2 * i:2 * i + 2, :], bank[:], ALU.add)\
                        .then_inc(free, 1)
                elif kind == "gu":
                    g = n["g"]
                    if g - 1 > 0:
                        dve.wait_ge(s_glo_done, g - 1)
                    dve.wait_ge(s_gate_th, n["gt"] + 1)
                    link(v.scalar_tensor_tensor(gate_t[:, g % 2, :], gate_t[:, g % 2, :], 1.0, bank[:, 0, :], ALU.add,
                                                ALU.mult))
                    v.scalar_tensor_tensor(hid[:, g % 2, :], gate_t[:, g % 2, :], 0.5, bank[:, 1, :], ALU.mult,
                                           ALU.mult).then_inc(s_hid_done, 1)
                    dve.wait_ge(s_hid_done, g + 1)
                    v.sem_inc(free, 1)
                elif kind == "mods":
                    dve.wait_ge(p2_ld, 16)
                    dve.wait_ge(s_mod_sb, L + 1)
                    for sub in range(3):
                        eight = slice(8 * sub, 8 * sub + 8)
                        v.scalar_tensor_tensor(s2["A"][:, eight], modv[:, L, sub, 1, :], 1.0,
                                               p2_(L, "pre")[:, eight], ALU.add, ALU.mult)
                        link(v.scalar_tensor_tensor(s2["B"][:, eight], modv[:, L, sub, 2, :], 1.0 if sub == 1 else 0.5,
                                                    p2_(L, "post")[:, eight], ALU.mult, ALU.mult))
                elif kind == "coef":
                    t = s2
                    TS, TTn, STT = v.tensor_scalar, v.tensor_tensor, v.scalar_tensor_tensor
                    dve.wait_ge(s_dt_done, L + 1)
                    link(TS(t["re"], p2_(L, "a_re"), -1e-4, None, ALU.min))
                    link(TTn(t["im"], p2_(L, "a_im"), t["dt"], ALU.mult))
                    link(TTn(t["l2"], t["re"], t["re"], ALU.mult))
                    link(TTn(t["t1"], p2_(L, "a_im"), p2_(L, "a_im"), ALU.mult))
                    link(TTn(t["l2"], t["l2"], t["t1"], ALU.add))
                    link(v.reciprocal(t["l2"], t["l2"]))
                    link(TTn(t["t2"], t["re"], t["l2"], ALU.mult))
                    link(STT(t["den"], p2_(L, "a_im"), -1.0, t["l2"], ALU.mult, ALU.mult))
                    TTn(t["re"], t["re"], t["dt"], ALU.mult).then_inc(s_co_dve, 1)
                    link(TS(t["ph"], t["im"], 0.15915494309189535, None, ALU.mult))
                    link(TS(t["t1"], t["ph"], ROUND, ROUND, ALU.add, ALU.subtract))
                    TTn(t["ph"], t["ph"], t["t1"], ALU.subtract).then_inc(s_co_dve, 1)
                    dve.wait_ge(s_co_act, L + 1)
                    link(TS(t["t1"], t["ta"], -1.0, 1.0, ALU.mult, ALU.add))
                    link(v.reciprocal(t["t1"], t["t1"]))
                    link(STT(t["em"], t["ta"], 2.0, t["t1"], ALU.mult, ALU.mult))
                    link(TS(t["r"], t["em"], 1.0, None, ALU.add))
                    link(TTn(t["cs"], t["sh"], t["sh"], ALU.mult))
                    link(TS(t["cs"], t["cs"], -2.0, None, ALU.mult))
                    link(TTn(t["t1"], t["em"], t["cs"], ALU.mult))
                    link(TTn(t["t1"], t["t1"], t["em"], ALU.add))
                    link(TTn(t["t1"], t["t1"], t["cs"], ALU.add))
                    link(TTn(t["sn"], t["sn"], t["r"], ALU.mult))
                    link(TTn(t["kr"], t["t1"], t["t2"], ALU.mult))
                    link(TTn(t["ki"], t["sn"], t["den"], ALU.mult))
                    link(TTn(t["kr"], t["kr"], t["ki"], ALU.subtract))
                    link(TTn(t["ki"], t["t1"], t["den"], ALU.mult))
                    link(TTn(t["sn"], t["sn"], t["t2"], ALU.mult))
                    link(TTn(t["ki"], t["ki"], t["sn"], ALU.add))
                    wide = lambda a: a.unsqueeze(2).to_broadcast([P, ST, 32])
                    cre, cim = (p2_(L, k).rearrange("p (s n) -> p s n", n=32) for k in ("c_re", "c_im"))
                    tmp = Bx["pa"].rearrange("p (s n) -> p s n", n=32)
                    link(TTn(cp[:, 0], cre, wide(t["kr"]), ALU.mult))
                    link(TTn(tmp, cim, wide(t["ki"]), ALU.mult))
                    link(TTn(cp[:, 0], cp[:, 0], tmp, ALU.subtract))
                    link(TTn(cp[:, 1], cre, wide(t["ki"]), ALU.mult))
                    link(TTn(tmp, cim, wide(t["kr"]), ALU.mult))
                    STT(Bx["cp"][:, 512:1024], Bx["cp"][:, 512:1024], -1.0, Bx["pa"], ALU.mult, ALU.subtract)\
                        .then_inc(s_cre_done, 1)
                    dve.wait_ge(s_cre_done, L + 1)
                elif kind == "pair" and B == 2 and i >= 8:
                    evacuated(dve, B, L, kind, i)
                    dst, t = (sga, i - 8) if i < 12 else (sgb, i - 12)
                    two = dst[:, 2 * t:2 * t + 2, :]
                    link(v.tensor_scalar(two, two, 0.5, 0.5, ALU.mult, ALU.add))
                elif kind == "ssm":
                    k = ST * L + i
                    r = s2["r"][:, i:i + 1]
                    if i == 0:
                        turns(0, k)
                    dve.wait_ge(s_tab_sin, k + 1)
                    dve.wait_ge(s_bu_sb, k + 1)
                    v.tensor_tensor(Bx["pa"], tab[:, i % 2, 256:768], bu[:, i % 2, :], ALU.mult)\
                        .then_inc(s_z_in, 1)
                    v.tensor_tensor(Bx["pb"], tab[:, i % 2, 0:512], bu[:, i % 2, :], ALU.mult)\
                        .then_inc(s_z_in, 1)
                    if i + 1 < ST:
                        turns(i + 1, k + 1)
                    dve.wait_ge(s_z_in, 2 * (k + 1))
                    v.tensor_tensor(Bx["z"][:, 0:T], Bx["pa"][:, 0:T], Bx["pa"][:, T:2 * T], ALU.add)
                    link(v.tensor_tensor(Bx["z"][:, T:2 * T], Bx["pb"][:, T:2 * T], Bx["pb"][:, 0:T], ALU.subtract))
                    if 2 * (k - 1) > 0:
                        dve.wait_ge(s_s_sum, 2 * (k - 1))
                    for e in range(2):
                        v.tensor_tensor_scan(wv[:, i % 2, e * T:(e + 1) * T], r.to_broadcast([P, T]),
                                             Bx["z"][:, e * T:(e + 1) * T], 0.0, ALU.mult, ALU.add)\
                            .then_inc(s_wv_done, 1)
                elif kind == "gelu":
                    dve.wait_ge(s_pe_y, ST * (L + 1))
                    dve.wait_ge(s_s_sum, 2 * ST * (L + 1))
                    for t in range(4):
                        link(v.scalar_tensor_tensor(G[:, 0, t * T:(t + 1) * T], u2[:, t, :], p2_(L, "d", t, t + 1),
                                                    work[2 + t // 2][:, (t % 2) * T:(t % 2 + 1) * T], ALU.mult, ALU.add))
                    v.tensor_scalar(G[:, 2, :], G[:, 0, :], 0.5, None, ALU.mult).then_inc(s_g_in, 1)
                    link(v.tensor_tensor(G[:, 1, :], G[:, 0, :], G[:, 0, :], ALU.mult))
                    v.tensor_scalar(G[:, 1, :], G[:, 1, :], 0.044715, 1.0, ALU.mult, ALU.add).then_inc(s_g_in, 1)
                    dve.wait_ge(s_g_in, 4 * L + 2)
                    v.tensor_tensor(G[:, 1, :], G[:, 1, :], G[:, 0, :], ALU.mult).then_inc(s_g_in, 2)
                    dve.wait_ge(s_g_tanh, L + 1)
                    for t in range(4):
                        g = n["g"] + t
                        dve.wait_ge(s_glo_done, g - 1)
                        v.scalar_tensor_tensor(hid[:, g % 2, :], G[:, 1, t * T:(t + 1) * T], 1.0,
                                               G[:, 2, t * T:(t + 1) * T], ALU.add, ALU.mult).then_inc(s_hid_done, 1)
                elif kind == "forget":
                    dve.wait_ge(s_pe_f, L + 1)
                    v.tensor_tensor(s2["f"].rearrange("p (c n) -> p c n", c=2),
                                    work[0][:, 0:16].rearrange("p (c n) -> p c n", c=2),
                                    p2_(L, "f_b").unsqueeze(1).to_broadcast([P, 2, 8]), ALU.add).then_inc(s_f_dve, 1)
                    dve.wait_ge(s_f_act, L + 1)
                    v.scalar_tensor_tensor(s2["lf"], s2["f"], 0.0, s2["ln"], ALU.min, ALU.subtract)\
                        .then_inc(s_lf_done, 1)
                    for j in range(AH // 2):
                        dve.wait_ge(s_pe_ck, 4 * L + j + 1)
                        if j == 0:
                            dve.wait_ge(s_hid_done, n["g"])
                        src = work[j][:].rearrange("p (h n) -> p h n", h=2)
                        for cols, sc_ in ((slice(0, T), slice(0, T)), (slice(T, T + P), slice(0, P))):
                            w_ = cols.stop - cols.start
                            v.tensor_tensor(cm[:, 2 * j:2 * j + 2, cols], src[:, :, sc_],
                                            c_("pen")[:, cols].unsqueeze(1).to_broadcast([P, 2, w_]), ALU.add)\
                                .then_inc(s_cm_done, 1)
                elif kind == "head":
                    dve.wait_ge(s_pe_sc, AH * L + i + 1)
                    if i == 0:
                        dve.wait_ge(s_cm_done, 8 * (L + 1))
                    v.scalar_tensor_tensor(lg[:, i % 2, :], work[i % 2][:, 0:384], float(AD) ** -0.5, cm[:, i, :],
                                           ALU.mult, ALU.subtract).then_inc(s_lg_done, 1)
                    dve.wait_ge(s_lg_done, AH * L + i + 1)
                    for e, cols in enumerate((slice(0, T), slice(T, T + P))):
                        v.tensor_reduce(s2["mxn"][:, 2 * i + e:2 * i + e + 1], lg[:, i % 2, cols], AX.X, ALU.max,
                                        negate=True).then_inc(s_nm_done, 1)
                    for k in ([i - 1] if i >= 1 else []) + ([i] if i == AH - 1 else []):
                        dve.wait_ge(s_p_exp, 2 * (AH * L + k + 1))
                        link(v.reciprocal(s2["rec"][:, 2 * k:2 * k + 2], s2["sum"][:, 2 * k:2 * k + 2]))
                        for e, cols in enumerate((slice(0, T), slice(T, T + P))):
                            v.tensor_scalar(pr[:, k % 2, cols], pr[:, k % 2, cols], s2["rec"][:, 2 * k + e:2 * k + e + 1],
                                            None, ALU.mult).then_inc(s_p_norm, 1)
                    for kp in {3: [0], 5: [1], 7: [2, 3]}.get(i, []):
                        dve.wait_ge(s_pe_at, AH * L + 2 * kp + 2)
                        v.tensor_copy(hf[:, kp, :], work[2 + kp % 2][:, 0:T]).then_inc(s_hf_done, 1)
                    if i == AH - 1:
                        for t in range(4):
                            low_h(n, t)
                elif kind == "aout":
                    two = sgb[:, 2 * i:2 * i + 2, :]
                    v.tensor_tensor(two, two, bank[:], ALU.mult).then_inc(free, 1)
                elif kind == "glu":
                    gt = gate_t[:, i % 2, :]
                    dve.wait_ge(s_gate_th, n["gt"] + 1)
                    v.scalar_tensor_tensor(gt, gt, 1.0, bank[:, 0, :], ALU.add, ALU.mult).then_inc(free, 1)
                    evacuated(dve, B, L, kind, i)
                    link(v.tensor_tensor(gt, gt, sga[:, i, :], ALU.mult))
                    if i % 2 == 0:
                        evacuated(dve, B, L, "aout", i // 2)
                    v.scalar_tensor_tensor(hf[:, i, :], gt, 0.5, sgb[:, i, :], ALU.mult, ALU.add)\
                        .then_inc(s_hf_done, 1)
                    low_h(n, i, first=i)
                elif kind == "mout":
                    v.tensor_copy(hf[:, 2 * i:2 * i + 2, :], bank[:]).then_inc(free, 1)

        @block.gpsimd
        def _(pool):
            v = nc.gpsimd

            def low_g(g, slot):
                pool.wait_ge(s_ghi_done, g + 1)
                v.tensor_tensor(g_lo[:, slot, :], hid[:, g % 2, :], g_hi[:, slot, :].bitcast(F32), ALU.subtract)\
                    .then_inc(s_glo_done, 1)

            pool.wait_ge(con_in, 16)
            for B, L, kind, i, n in NUMBERED:
                if kind == "gates":
                    pool.wait_ge(s_gates_done, L + 1)
                    for r in range(8):
                        v.tensor_scalar(lts[:, r, :], ident, sm["beta"][:, r:r + 1], None, ALU.mult)\
                            .then_inc(s_pool_db, 1)
                elif kind == "decay":
                    for c in range(TT):
                        pool.wait_ge(s_dec_done, 2 * L + c + 1)
                        four = dec[:, 4 * c:4 * c + 4, :]
                        v.tensor_tensor(four, four, triu.unsqueeze(1).to_broadcast([P, 4, P]), ALU.mult)\
                            .then_inc(s_decm_done, 1)
                elif kind == "qknorm":
                    pool.wait_ge(s_qk_ready, 4 * L + 2)
                    pool.wait_ge(s_silu_done, 6 * (L + 1))
                    pool.wait_ge(s_egr_done, L + 1)
                    v.tensor_tensor(qdec, qT[:, :, P:T], egr.rearrange("p (n t) -> p n t", t=P), ALU.mult)\
                        .then_inc(s_qdec_done, 1)
                elif kind in ("kk", "level") and i < 6:
                    lev = 1 if kind == "kk" else i + 1
                    if kind == "level" and i == 0:
                        continue
                    for c in range(TT):
                        pool.wait_ge(s_lt_done, 2 * L + c + 1)
                        if lev > 1:
                            pool.wait_ge(s_pe_t, 12 * L + 2 * (lev - 2) + c + 1)
                        v.tensor_tensor(lts[:, 4 * c:4 * c + 4, :], lt[:, 4 * c:4 * c + 4, :],
                                        c_("m", lev * P, (lev + 1) * P).unsqueeze(1).to_broadcast([P, 4, P]), ALU.mult)\
                            .then_inc(s_pool_lts, 1)
                elif kind == "gu":
                    low_g(n["g"], i % 4)
                elif kind == "gelu":
                    for t in range(4):
                        low_g(n["g"] + t, t)
                elif kind == "ssm":
                    k = ST * L + i
                    if i == 0:
                        pool.wait_ge(s_tab_arg, k + 1)
                        v.tensor_tensor(Bx["arg"], Bx["arg"], Bx["rnd"], ALU.subtract).then_inc(s_tab_frac, 1)
                    if i + 1 < ST:
                        pool.wait_ge(s_tab_arg, k + 2)
                        v.tensor_tensor(Bx["arg"], Bx["arg"], Bx["rnd"], ALU.subtract).then_inc(s_tab_frac, 1)
                    pool.wait_ge(s_wv_done, 2 * (k + 1))
                    if 2 * k > 0:
                        pool.wait_ge(s_s_sum, 2 * k)
                    v.tensor_tensor(Bx["pc"], tab[:, i % 2, 256:768], wv[:, i % 2, :], ALU.mult).then_inc(s_ab_done, 1)
                    v.tensor_tensor(Bx["pd"], tab[:, i % 2, 0:512], wv[:, i % 2, :], ALU.mult).then_inc(s_ab_done, 1)
                    pool.wait_ge(s_ab_done, 2 * (k + 1))
                    if k - 1 > 0:
                        pool.wait_ge(s_pe_y, k - 1)
                    v.tensor_tensor(sst[:, i % 2, 0:T], Bx["pc"][:, 0:T], Bx["pc"][:, T:2 * T], ALU.subtract)\
                        .then_inc(s_s_sum, 1)
                    v.tensor_tensor(sst[:, i % 2, T:2 * T], Bx["pd"][:, 0:T], Bx["pd"][:, T:2 * T], ALU.add)\
                        .then_inc(s_s_sum, 1)


def kernel(**inputs):
    import concourse.bacc as bacc
    from concourse.bass_utils import run_bass_kernel_spmd

    a = {k: np.asarray(v) for k, v in inputs.items()}
    f32 = np.float32

    def unit_of_columns(w_, c0):
        return w_[:, c0:c0 + P].reshape(DT, P, P).transpose(1, 0, 2).reshape(P, UNIT)

    def unit_of_two(w_, c0, c1):
        both = np.stack([w_[:, c0:c0 + P], w_[:, c1:c1 + P]])
        return both.reshape(2, 4, P, P).transpose(2, 0, 1, 3).reshape(P, UNIT)

    units = []
    ffn = 0
    for B, L, kind, i in STEPS:
        if kind == "pre":
            ffn = i // 2
        if B == 1:
            gate, up, down = a["ffn_w_gate"][L], a["ffn_w_up"][L], a["ffn_w_down"][L]
        else:
            both = a["ffn_w_in_2"][L, ffn]
            gate, up, down = both[:, :FT * P], both[:, FT * P:], a["ffn_w_out_2"][L, ffn]
        if kind == "mod":
            units += [unit_of_columns(a["mod_w_2"][L], (2 * i + e) * P) for e in range(2)]
        elif kind == "pair" and B == 1:
            c0 = 4 * HEADS * HD + 2 * HEADS
            cols = [256 * i, 256 * i + P] if i < 8 else \
                [c0 + 512 + (i - 8) * P, c0 + 1024 + (i - 8) * P] if i < 12 else \
                [c0 + 256 * (i - 12), c0 + 256 * (i - 12) + P]
            units += [unit_of_columns(a["w_in"][L], c) for c in cols]
        elif kind == "pair":
            c0 = 256 * i if i < 8 else 4 * 512 + AH + 256 * (i - 8)
            units += [unit_of_columns(a["mix_w_in_2"][L], c0 + e * P) for e in range(2)]
        elif kind in ("out", "mout"):
            w_ = a["w_out"][L] if kind == "out" else a["mix_w_out_2"][L]
            units += [unit_of_columns(w_, (2 * i + e) * P) for e in range(2)]
        elif kind == "gu":
            units += [unit_of_columns(gate, i * P), unit_of_columns(up, i * P)]
        elif kind == "down":
            units += [down[(2 * i + e) * P:(2 * i + e + 1) * P, :] for e in range(2)]
        elif kind == "aout":
            units.append(unit_of_two(a["attn_w_out_2"][L], 2 * i * P, (2 * i + 1) * P))
        elif kind == "glu":
            units.append(unit_of_two(a["glu_w_2"][L], i * P, D + i * P))
    w = np.stack(units).reshape(-1, 2, P, UNIT).transpose(0, 2, 1, 3).reshape(-1, P, 2 * UNIT)

    def tiles(vec):
        return vec.reshape(-1, P).T

    def rows(vec):
        return np.broadcast_to(vec.reshape(1, -1), (P, vec.size))

    def pack(cols, n, parts):
        out_ = np.zeros((P, n), f32)
        for name, (lo, hi) in cols.items():
            out_[:, lo:hi] = parts[name]
        return out_

    idx = np.arange(P)
    same = lambda size: (idx[:, None] // size) == (idx[None, :] // size)
    masks = [same(2 * z) & ~same(z) & (idx[:, None] < idx[None, :]) for z in (1, 2, 4, 8, 16, 32, 64)]
    future = np.where(idx[None, :] > idx[:, None], BIG, 0.0)
    const = pack(PC, NC, {
        "ident": np.eye(P), "triu": (idx[:, None] <= idx[None, :]), "ones": np.ones((P, P)),
        "m": np.concatenate(masks, axis=1), "pen": np.concatenate([np.zeros((P, P)), future, future], axis=1),
        "time": np.broadcast_to(np.arange(T)[None, :], (P, T)), "c": tiles(a["c_2"][0]),
        "final": tiles(a["final_norm_g"])})

    w_in = a["w_in"]
    lo = 4 * HEADS * HD
    p1 = np.stack([pack(P1, N1, {
        "norm1": tiles(a["norm1_g"][L]), "norm2": tiles(a["norm2_g"][L]),
        "conv": a["dn_conv_w"][L].reshape(TAPS, 12, P).transpose(2, 1, 0).reshape(P, -1),
        "sconv": a["sc_conv_w"][L].reshape(STAPS, 4, P).transpose(2, 1, 0).reshape(P, -1),
        "dn_g": tiles(a["dn_norm_g"][L]), "sc_g": tiles(a["sc_norm_g"][L]),
        "w_ba": w_in[L][:, lo:lo + 8].reshape(DT, P, 8).transpose(1, 0, 2).reshape(P, -1),
        "dt_bias": rows(a["dn_dt_bias"][L]), "a_log": rows(a["dn_a_log"][L]),
        "mod_b": tiles(a["mod_b_2"][L])}) for L in range(LAYERS)], axis=1)

    def ssm_b(b):
        out_ = np.zeros((P, 4, P), f32)
        for ut in range(4):
            for j in range(4):
                for g in range(2):
                    out_[32 * j + 16 * g:32 * j + 16 * g + 16, ut, 64 * g:64 * g + 64] = b[ut * 8 + 2 * j + g].T
        return out_.reshape(P, -1)

    def ssm_c(c):
        out_ = np.zeros((P, ST, 32), f32)
        for st in range(ST):
            for g in range(2):
                out_[64 * g:64 * g + 64, st, 16 * g:16 * g + 16] = c[2 * st + g].T
        return out_.reshape(P, -1)

    p2 = np.stack([pack(P2, N2, {
        "pre": tiles(a["norm_pre_2"][L].reshape(-1)), "post": tiles(a["norm_post_2"][L].reshape(-1)),
        "w_f": a["mix_w_in_2"][L][:, 2048:2056].reshape(DT, P, 8).transpose(1, 0, 2).reshape(P, -1),
        "f_b": rows(a["forget_b_2"][L]), "a_re": tiles(a["ssm_a_re_2"][L].reshape(-1)),
        "a_im": tiles(a["ssm_a_im_2"][L].reshape(-1)), "log_dt": tiles(np.repeat(a["ssm_log_dt_2"][L], SP_)),
        "d": tiles(a["ssm_d_2"][L]), "b_re": ssm_b(a["ssm_b_re_2"][L]), "b_im": ssm_b(a["ssm_b_im_2"][L]),
        "c_re": ssm_c(a["ssm_c_re_2"][L]), "c_im": ssm_c(a["ssm_c_im_2"][L])}) for L in range(LAYERS)], axis=1)

    def feature_major(m):
        return m.T.reshape(DT, P, T).transpose(1, 0, 2)

    ins = {"w": w, "x_in": feature_major(a["x"][0]), "const_in": const, "p1_in": p1, "p2_in": p2}
    ins = {k: np.ascontiguousarray(v) for k, v in ins.items()}
    nc = bacc.Bacc("TRN2", target_bir_lowering=False, num_devices=1)
    aps = [nc.dram_tensor(k, v.shape, F32, kind="ExternalInput").ap() for k, v in ins.items()]
    out = nc.dram_tensor("out", (P, DT, T), F32, kind="ExternalOutput").ap()
    build(nc, *aps, out)
    res = run_bass_kernel_spmd(nc, [ins], core_ids=[0]).results[0]["out"]
    return np.ascontiguousarray(res.transpose(1, 0, 2).reshape(D, T).T)[None]
```

```python
from contextlib import ExitStack

import numpy as np

import concourse.bass as bass
from concourse import mybir

F32 = mybir.dt.float32
F32R = mybir.dt.float32r
ALU = mybir.AluOpType
ACT = mybir.ActivationFunctionType
AX = mybir.AxisListType

P = 128
T = 256
TT = T // P
D = 1024
DT = D // P
LAYERS = 2
EPS = 1e-6
HEADS, HD = 4, 128
TAPS, STAPS = 4, 3
AH, AD = 8, 64
SG, SN, SP_ = 32, 16, 64
ST = SG * SP_ // P
FT = 2816 // P
MODT = 72
BIG = 1e30
ROUND = 12582912.0

UNIT = 8 * P
RAWS = 4
SLOTS = 4

COEF = 5


def ffn_order():
    out = [("gu", 0), ("gu", 1)]
    for j in range(FT // 2):
        if 2 * j + 2 < FT:
            out.append(("gu", 2 * j + 2))
        out.append(("down", j))
        if 2 * j + 3 < FT:
            out.append(("gu", 2 * j + 3))
    return out


FIRST = (
    [("norm", 0), ("pair", 0), ("crow", 0), ("gates", 0), ("pair", 1), ("decay", 0), ("pair", 2), ("brow", 0),
     ("pair", 3), ("pair", 4), ("pair", 5), ("pair", 6), ("qknorm", 0), ("pair", 7), ("pair", 8), ("kk", 0),
     ("pair", 9), ("tok", 0), ("level", 0), ("level", 1)]
    + [s for i in range(4) for s in (("pair", 10 + i), ("level", i + 2))] + [("level", 6)]
    + [("scnorm", 0), ("scan", 0), ("headnorm", 0)]
    + [("out", j) for j in range(DT // 2)] + [("norm", 1)] + ffn_order() + [("acc", 0)]
)
SECOND = (
    [("mods", 0), ("pre", 0)] + ffn_order()[:8]
    + [s for i, step in enumerate(ffn_order()[8:8 + COEF]) for s in (("coef", i), step)] + ffn_order()[8 + COEF:]
    + [("post", 0), ("pre", 1), ("pair", 0), ("flog", 0), ("pair", 1)]
    + [s for i in range(12) for s in (("ssm", i), ("pair", 2 + i))]
    + [("ssm", 12), ("ssm", 13), ("pair", 14), ("ssm", 14), ("ssm", 15), ("pair", 15), ("gelu", 0)]
    + [("forget", 0), ("vtok", 0)] + [s for h in range(AH) for s in (("head", h), ("glu", h))]
    + [("aout", j) for j in range(4)]
    + [("mout", j) for j in range(DT // 2)] + [("post", 1), ("pre", 2)] + ffn_order() + [("post", 2)]
)


def with_mod(steps):
    def room(s):
        if s[2] in ("level", "out"):
            return 2 if s[2:] in (("level", 2), ("level", 3), ("level", 4), ("out", 0), ("out", 1)) else 0
        return ({"down": 2} if s[0] == 1 else {"down": 3, "gu": 1, "mout": 1}).get(s[2], 0)

    n, done, seen, out = sum(room(s) for s in steps), 0, 0, []
    for s in steps:
        out.append(s)
        if room(s):
            seen += room(s)
            while done < (MODT // 2) * seen // n:
                out.append((s[0], s[1], "mod", done))
                done += 1
    return out + [(s[0], s[1], "modsum", 0)]


STEPS = with_mod([(1, L, kind, i) for L in range(LAYERS) for kind, i in FIRST if (kind, L) != ("crow", 1)]) + \
        [(1, LAYERS - 1, "final", 0)] + with_mod([(2, 0, kind, i) for kind, i in SECOND]) + \
        [(2, 1, kind, i) for kind, i in SECOND]
UNITS_OF = {"pair": 2, "out": 2, "mout": 2, "gu": 2, "down": 2, "aout": 1, "glu": 1}


def numbered():
    n = dict(split=0, pair=0, norm=0, h=0, g=0, gt=0, sq=0, x=0, y=0, mod=0)
    out = []
    for B, L, kind, i in STEPS:
        out.append((B, L, kind, i, dict(n)))
        n["mod"] += kind == "mod"
        n["split"] += UNITS_OF.get(kind, 0)
        n["pair"] += kind in ("pair", "out", "mout", "gu", "aout", "glu")
        n["norm"] += kind in ("norm", "pre", "post", "final")
        n["h"] += {"norm": 8, "pre": 8, "scnorm": 4, "headnorm": 4, "aout": 2}.get(
            kind, 4 if (kind, i) == ("head", AH - 1) else 0)
        n["g"] += {"gu": 1, "gelu": 4}.get(kind, 0)
        n["gt"] += kind in ("gu", "glu")
        n["sq"] += {"scnorm": 2, "headnorm": 2}.get(
            kind, 4 if kind in ("norm", "pre", "post", "final", "qknorm") else 0)
        n["x"] += {"acc": 4, "post": 4, "final": 8}.get(kind, 0)
        n["y"] += 8 if kind == "post" else 0
    return out, n


NUMBERED, TOTAL = numbered()
AT = {(B, L, kind, i): n for B, L, kind, i, n in NUMBERED}


def columns(sizes):
    at, out = 0, {}
    for name, n in sizes:
        out[name] = (at, at + n)
        at += n
    return out, at


P1, N1 = columns([("norm1", 8), ("norm2", 8), ("conv", 12 * TAPS), ("sconv", 4 * STAPS), ("dn_g", 1), ("sc_g", 4),
                  ("w_ba", 8 * 8), ("dt_bias", 4), ("a_log", 4), ("mod_b", MODT)])
P2, N2 = columns([("pre", 24), ("post", 24), ("w_f", 8 * 8), ("f_b", 8), ("a_re", ST), ("a_im", ST), ("log_dt", ST),
                  ("d", 4), ("b_re", 4 * P), ("b_im", 4 * P), ("c_re", ST * 32), ("c_im", ST * 32)])
PC, NC = columns([("ident", P), ("triu", P), ("ones", P), ("m", 7 * P), ("pen", 3 * P), ("time", T), ("c", 8),
                  ("final", 8)])
MXN = 17912


def build(nc, w, x_in, const_in, p1_in, p2_in, out):
    with ExitStack() as ctx:
        def sb(name, shape, dt=F32):
            return ctx.enter_context(nc.sbuf_tensor(name, shape, dt))

        def ps(name, shape):
            return ctx.enter_context(nc.psum_tensor(name, shape, F32))

        def sem(name):
            return ctx.enter_context(nc.semaphore(name))

        raw = sb("raw", [P, RAWS, 2 * UNIT])
        w_hi = sb("w_hi", [P, SLOTS, UNIT], F32R)
        w_lo = sb("w_lo", [P, SLOTS, UNIT], F32R)
        x = sb("x", [P, DT, T])
        hf = sb("hf", [P, DT, T])
        h_hi = sb("h_hi", [P, DT, T], F32R)
        h_lo = sb("h_lo", [P, DT, T], F32R)
        g_hi = sb("g_hi", [P, 4, T], F32R)
        g_lo = sb("g_lo", [P, 4, T], F32R)
        hid = sb("hid", [P, 2, T])
        gate_t = sb("gate_t", [P, 2, T])
        sq = sb("sq", [P, 2, 2 * T])
        rstd = sb("rstd", [P, T])
        std = sb("std", [P, T])
        con = sb("con", [P, NC])
        par1 = sb("par1", [P, LAYERS, N1])
        par2 = sb("par2", [P, N2])
        modv = sb("modv", [P, LAYERS, 3, 3, DT])
        modacc = sb("modacc", [P, MODT])
        crow = sb("crow", [P, D])
        csil = sb("csil", [P, 2, DT])
        mx = sb("mx", [P, MXN])

        stream = [ps(f"stream{i}", [P, 2, T]) for i in range(2)]
        work = [ps(f"work{i}", [P, 512]) for i in range(4)]
        stat = ps("stat", [P, 512])
        turned = ps("turned", [P, 512])

        def view(tensor, cols, name, lo, hi):
            a, b = cols[name]
            return tensor[:, a + lo:(b if hi is None else a + hi)]

        def c_(name, lo=0, hi=None):
            return view(con, PC, name, lo, hi)

        def p1_(L, name, lo=0, hi=None):
            return view(par1[:, L, :], P1, name, lo, hi)

        def p2_(L, name, lo=0, hi=None):
            return view(par2[:], P2, name, lo, hi)

        ident, triu, ones = c_("ident"), c_("triu"), c_("ones")
        triu_ones = con[:, PC["triu"][0]:PC["ones"][1]]

        def carve(whole, sizes, limit):
            cols, n = columns(sizes)
            assert n <= limit, (n, limit)
            return {k: whole[:, a:b] for k, (a, b) in cols.items()}

        A = carve(mx, [("q", 1024), ("k", 1024), ("v", 1024), ("rawp", 2 * 2 * 259), ("y", 1024), ("th", 1024),
                       ("z", 1024), ("scp", 4 * 258), ("sc", 1024), ("dec", 1024), ("lt", 1024), ("qk", 1024),
                       ("xt", 1024), ("x", 1024), ("lts", 1024), ("t", 1024), ("kd", 1024),
                       ("small", 160)], MXN)
        qT, kT, vT, yv, th, zs, sc = (A[k].rearrange("p (n t) -> p n t", t=T) for k in
                                      ("q", "k", "v", "y", "th", "z", "sc"))
        dec, lt, qk, xt, xi, lts, tt, kd, vb = (A[k].rearrange("p (n t) -> p n t", t=P) for k in
                                                ("dec", "lt", "qk", "xt", "x", "lts", "t", "kd", "v"))
        rawp = A["rawp"].rearrange("p (b i t) -> p b i t", b=2, i=2)
        scp = A["scp"].rearrange("p (n t) -> p n t", n=4)
        egr = A["x"][:, 0:512]
        qdec = A["y"][:, 0:512].rearrange("p (n t) -> p n t", t=P)
        sd = [A["t"][:, 0:512], A["t"][:, 512:1024], A["kd"][:, 0:512], A["kd"][:, 512:1024]]
        scd = [A["th"][:, 0:512], A["th"][:, 512:1024]]
        vn0, s_sb = lts[:, 0:4, :], lts[:, 4:8, :]
        w_sb, vn1 = tt[:, 0:4, :], tt[:, 4:8, :]
        sm = carve(A["small"], [("ba", 16), ("ap", 8), ("tb", 8), ("beta", 8), ("hb", 8), ("ab", 8), ("ln", 8),
                                ("ea", 4), ("g", 8), ("gc", 16), ("eg", 8), ("ekd", 8), ("d", 8), ("bke", 8),
                                ("sp", 8)], 160)

        Bx = carve(mx, [("u", 1024), ("q", 1024), ("k", 1024), ("v", 1024), ("sga", 2048), ("sgb", 2048),
                        ("tab", 1536), ("arg", 512), ("rnd", 512), ("bu", 1024), ("pa", 512), ("pb", 512), ("pc", 512),
                        ("pd", 512), ("z", 512), ("wv", 1024), ("s", 1024), ("cp", 1024), ("small", 500)], MXN)
        u2, q2, k2, v2, sga, sgb = (Bx[k].rearrange("p (n t) -> p n t", t=T) for k in
                                    ("u", "q", "k", "v", "sga", "sgb"))
        tab = Bx["tab"].rearrange("p (b n) -> p b n", b=2)
        bu, wv, sst = (Bx[k].rearrange("p (b n) -> p b n", b=2) for k in ("bu", "wv", "s"))
        cp = Bx["cp"].rearrange("p (b s n) -> p b s n", b=2, n=32)
        a0, b0 = columns([("u", 1024), ("q", 1024), ("k", 1024), ("v", 1024), ("sga", 2048), ("sgb", 2048)])[1], 3072
        cm = mx[:, a0:a0 + b0].rearrange("p (h n) -> p h n", n=384)
        G = mx[:, a0:a0 + 3072].rearrange("p (b n) -> p b n", b=3)
        a1 = a0 + 3584
        lg, pr, pt = (mx[:, a1 + 768 * j:a1 + 768 * (j + 1)].rearrange("p (b n) -> p b n", b=2) for j in range(3))
        vt = Bx["u"].rearrange("p (c n) -> p c n", c=2)
        s2 = carve(Bx["small"], [("A", 24), ("B", 24)] + [(k, 16) for k in
                   ("dt", "re", "im", "ta", "r", "em", "den", "ph", "sh", "sn", "l2", "kr", "ki", "t1", "t2", "f", "ab",
                    "ln", "lf", "mxn", "sum", "rec", "cs")], 500)

        (s_mod_used, s_hi_ready, s_lo_ready, s_unit_done, s_bank0, s_bank1) = (
            sem(n) for n in "mod_used hi_ready lo_ready unit_done bank0 bank1".split())
        (s_pe_stat, s_sq_done, s_sqrt_done, s_hf_done, s_hhi_done, s_hlo_done, s_gate_th, s_hid_done,
         s_ghi_done, s_glo_done, s_x_done, s_y_scaled, s_shifted, s_mod_sb, s_c_th, s_csil_done, s_pe_crow, s_crow_done,
         s_glu_done, s_dve_self,
         s_act_self, s_pe_ba, s_ba_ap, s_act_ap, s_gates_done, s_pe_gc, s_gc_sb, s_dd_done, s_act_eg,
         s_pe_grow, s_dpre, s_egr_done, s_dec_done, s_decm_done, s_pool_db, s_pe_brow, s_lt_half,
         s_conv_done, s_th_done, s_silu_done, s_qk_sqrt, s_qk_ready, s_pe_kk, s_lt_done, s_qk_done,
         s_pe_tok, s_kd_done, s_vb_done, s_xt_done, s_pool_lts, s_pe_x0, s_x0_sb, s_pe_t, s_t_sb, s_pe_dx,
         s_x_upd, s_z_th, s_c_done, s_pe_u0, s_vn0_done, s_pe_s, s_s_done, s_pe_w, s_w_done, s_pe_u1,
         s_vn1_done, s_qdec_done, s_pe_o, s_os_sqrt, s_ab_done, s_co_dve, s_co_act, s_cre_done, s_tab_arg,
         s_tab_frac, s_tab_sin, s_pe_bu, s_bu_sb, s_z_in, s_wv_done, s_s_sum, s_pe_y, s_g_in, s_g_tanh,
         s_pe_f, s_f_dve, s_f_act, s_lf_done, s_pe_ck, s_cm_done, s_pe_vt, s_vt_sb, s_pe_sc, s_lg_done,
         s_nm_done, s_p_exp, s_p_norm, s_pe_pt, s_pt_sb, s_pe_at, s_pads, s_dt_done) = (
            sem(n) for n in """pe_stat sq_done sqrt_done hf_done hhi_done hlo_done gate_th hid_done ghi_done glo_done
            x_done y_scaled shifted mod_sb c_th csil_done pe_crow crow_done glu_done dve_self act_self pe_ba ba_ap act_ap gates_done
            pe_gc gc_sb dd_done act_eg pe_grow dpre egr_done dec_done decm_done pool_db pe_brow
            lt_half conv_done th_done silu_done qk_sqrt qk_ready pe_kk lt_done qk_done pe_tok
            kd_done vb_done xt_done pool_lts pe_x0 x0_sb pe_t t_sb pe_dx x_upd z_th c_done pe_u0
            vn0_done pe_s s_done pe_w w_done pe_u1 vn1_done qdec_done pe_o os_sqrt ab_done co_dve
            co_act cre_done tab_arg tab_frac tab_sin pe_bu bu_sb z_in wv_done s_sum pe_y g_in g_tanh
            pe_f f_dve f_act lf_done pe_ck cm_done pe_vt vt_sb pe_sc lg_done nm_done p_exp p_norm
            pe_pt pt_sb pe_at pads dt_done""".split())
        banks = [s_bank0, s_bank1]
        loaded = [sem(f"loaded{i}") for i in range(RAWS)]
        con_in, x_ld, p1_ld, p2_ld, stored = (sem(n) for n in ("con_in", "x_ld", "p1_ld", "p2_ld", "stored"))

        chunks = []
        for B, L, kind, i, n in NUMBERED:
            if kind == "mod":
                chunks.append(("mod", n["mod"] + 1))
            else:
                for v in range(n["split"], n["split"] + UNITS_OF.get(kind, 0)):
                    if v % 2 == 0:
                        chunks.append(("split", v + 2))
        chunk_of_unit = [c for c, (kind, _) in enumerate(chunks) if kind == "split" for _ in range(2)]
        chunk_of_mod = [c for c, (kind, _) in enumerate(chunks) if kind == "mod"]

        def evacuated(e, *step):
            p = AT[step]["pair"]
            e.wait_ge(banks[p % 2], p // 2 + 1)

        def arrived(e, chunk):
            e.wait_ge(loaded[chunk % RAWS], 16 * (chunk // RAWS + 1))

        block = ctx.enter_context(nc.Block())

        @block.sync
        def _(sp):
            sp.dma_start(con[:], const_in).then_inc(con_in, 16)
            sp.dma_start(x[:], x_in).then_inc(x_ld, 16)
            sp.dma_start(par1[:], p1_in).then_inc(p1_ld, 16)
            for c in range(len(chunks)):
                if c >= RAWS:
                    kind, n = chunks[c - RAWS]
                    if kind == "mod":
                        sp.wait_ge(s_mod_used, 2 * n)
                    else:
                        sp.wait_ge(s_lo_ready, n)
                sp.dma_start(raw[:, c % RAWS, :], w[c]).then_inc(loaded[c % RAWS], 16)
                if c == 6:
                    sp.dma_start(par2[:], p2_in[:, 0, :]).then_inc(p2_ld, 16)
                if c == chunk_of_unit[AT[2, 0, "mout", 0]["split"]]:
                    sp.wait_ge(p2_ld, 16)
                    sp.wait_ge(s_cm_done, 8)
                    sp.dma_start(par2[:], p2_in[:, 1, :]).then_inc(p2_ld, 16)
            for j in range(4):
                sp.wait_ge(s_x_done, TOTAL["x"] - 4 + j + 1)
                sp.dma_start(out[:, 2 * j:2 * j + 2, :], x[:, 2 * j:2 * j + 2, :]).then_inc(stored, 16)
            sp.wait_ge(stored, 16 * 4)

        @block.tensor
        def _(pe):
            mm, tr = nc.tensor.matmul, nc.tensor.transpose

            def product(unit, blocks, r_hi, r_lo):
                slot = unit % SLOTS
                pe.wait_ge(s_lo_ready, unit + 1)
                for b, (o, kt, first, end) in enumerate(blocks):
                    hi = w_hi[:, slot, b * P:(b + 1) * P]
                    lo = w_lo[:, slot, b * P:(b + 1) * P]
                    mm(o, hi, r_hi[:, kt, :], start=first, stop=False, skip_group_check=True)
                    mm(o, hi, r_lo[:, kt, :], start=False, stop=False, skip_group_check=True)
                    last = mm(o, lo, r_hi[:, kt, :], start=False, stop=end, skip_group_check=True)
                last.then_inc(s_unit_done, 1)

            def attend(L, k, h0):
                kp, ke = k // 2, k % 2
                pe.wait_ge(s_pt_sb, AH * L + k + 1)
                if kp >= 2:
                    pe.wait_ge(s_hf_done, h0 + kp - 1)
                o = work[2 + kp % 2]
                orow = slice(64 * ke, 64 * ke + 64)
                mm(o[orow, 0:T], vt[:, 0, k * AD:(k + 1) * AD], pt[:, k % 2, 0:T], start=True, stop=False,
                   skip_group_check=True)
                mm(o[orow, P:T], vt[:, 1, k * AD:(k + 1) * AD], pt[:, k % 2, T:T + P], start=False, stop=True,
                   skip_group_check=True).then_inc(s_pe_at, 1)

            def heads(c):
                return [(h, c * HEADS + h, slice(h * P, (h + 1) * P)) for h in range(HEADS)]

            def sum_squares(n):
                for j in range(4):
                    pe.wait_ge(s_sq_done, n + j + 1)
                    for e in range(2):
                        last = mm(stat[:, 0:T], ones, sq[:, j % 2, e * T:(e + 1) * T], start=(j == 0 and e == 0),
                                  stop=(j == 3 and e == 1))
                    last.then_inc(s_pe_stat, 1)

            pe.wait_ge(con_in, 16)
            pe.wait_ge(p1_ld, 16)
            for B, L, kind, i, n in NUMBERED:
                bank = stream[n["pair"] % 2]
                if kind in ("pair", "out", "mout", "gu"):
                    if n["pair"] // 2 > 0:
                        pe.wait_ge(banks[n["pair"] % 2], n["pair"] // 2)
                    if i == 0:
                        pe.wait_ge(s_lo_ready, n["split"] + 2)
                        order = [4, 5, 6, 7, 0, 1, 2, 3] if kind in ("out", "mout") else list(range(DT))
                        for k, kt in enumerate(order):
                            pe.wait_ge(s_hlo_done, n["h"] - DT + k + 1)
                            for e in range(2):
                                slot = (n["split"] + e) % SLOTS
                                hi = w_hi[:, slot, kt * P:(kt + 1) * P]
                                lo = w_lo[:, slot, kt * P:(kt + 1) * P]
                                o = bank[:, e, :]
                                mm(o, hi, h_hi[:, kt, :], start=k == 0 and e == 0, stop=False, skip_group_check=True)
                                mm(o, hi, h_lo[:, kt, :], start=False, stop=False, skip_group_check=True)
                                last = mm(o, lo, h_hi[:, kt, :], start=False, stop=k == DT - 1,
                                          skip_group_check=True)
                                if k == DT - 1:
                                    last.then_inc(s_unit_done, 1)
                        continue
                    for e in range(2):
                        product(n["split"] + e, [(bank[:, e, :], kt, kt == 0, kt == DT - 1) for kt in range(DT)],
                                h_hi, h_lo)
                elif kind in ("aout", "glu"):
                    pe.wait_ge(banks[n["pair"] % 2], n["pair"] // 2)
                    if kind == "aout":
                        pe.wait_ge(s_hlo_done, AT[2, L, "aout", 0]["h"])
                    else:
                        pe.wait_ge(s_glo_done, AT[2, L, "gelu", 0]["g"] + 4)
                    product(n["split"], [(bank[:, m, :], kt, kt == 0, kt == 3) for m in range(2) for kt in range(4)],
                            h_hi if kind == "aout" else g_hi, h_lo if kind == "aout" else g_lo)
                    if kind == "glu" and 1 <= i < AH - 1:
                        attend(L, i - 1, n["h"])
                elif kind == "down":
                    for e in range(2):
                        row = 2 * i + e
                        base = n["g"] - min(2 * i + 3, FT)
                        pe.wait_ge(s_glo_done, base + row + 1)
                        product(n["split"] + e,
                                [(work[m // 2][:, (m % 2) * T:(m % 2 + 1) * T], row % 4, row == 0 and m % 2 == 0,
                                  row == FT - 1) for m in range(DT)], g_hi, g_lo)
                elif kind == "crow":
                    pe.wait_ge(s_csil_done, 1)
                    for half, dst in enumerate((turned, work[3])):
                        for j in range(4):
                            kt = 4 * half + j
                            last = mm(dst[:, j * P:(j + 1) * P], csil[:, 1, kt:kt + 1].to_broadcast([P, P]), ident,
                                      start=True, stop=True)
                        last.then_inc(s_pe_crow, 1)
                elif kind in ("norm", "pre", "post", "final"):
                    sum_squares(n["sq"])
                elif kind == "gates":
                    pe.wait_ge(s_hf_done, n["h"])
                    for c in range(TT):
                        for kt in range(DT):
                            last = mm(work[0][:, c * 8:c * 8 + 8], hf[:, kt, c * P:(c + 1) * P],
                                      p1_(L, "w_ba", kt * 8, kt * 8 + 8), start=(kt == 0), stop=(kt == DT - 1))
                    last.then_inc(s_pe_ba, 1)
                elif kind == "decay":
                    pe.wait_ge(s_gates_done, L + 1)
                    mm(work[1][:, 0:8], triu, sm["g"], start=True, stop=True)
                    mm(work[1][:, 8:16], ones, sm["g"], start=True, stop=True).then_inc(s_pe_gc, 1)
                    for c in range(TT):
                        for h, r, cols in heads(c):
                            last = mm(work[2 + c][:, cols], sm["g"][:, r:r + 1].to_broadcast([P, P]), triu,
                                      start=True, stop=True)
                        last.then_inc(s_pe_grow, 1)
                elif kind == "brow":
                    pe.wait_ge(s_pool_db, 8 * (L + 1))
                    pe.wait_ge(s_gc_sb, L + 1)
                    for c in range(TT):
                        for h, r, cols in heads(c):
                            last = mm(work[c][:, cols], ones, lts[:, r, :], start=True, stop=True)
                        last.then_inc(s_pe_brow, 1)
                elif kind == "qknorm":
                    pe.wait_ge(s_lt_half, 2 * (L + 1))
                    pe.wait_ge(s_dpre, 8 * (L + 1))
                    pe.wait_ge(s_egr_done, L + 1)
                    for j in range(4):
                        pe.wait_ge(s_sq_done, n["sq"] + j + 1)
                        mm(work[j][:], ones, sq[:, j % 2, :], start=True, stop=True).then_inc(s_pe_stat, 1)
                elif kind == "kk":
                    pe.wait_ge(s_qk_ready, 4 * (L + 1))
                    for c in range(TT):
                        for h, r, cols in heads(c):
                            kc = kT[:, h, c * P:(c + 1) * P]
                            mm(work[c][:, cols], kc, kc, start=True, stop=True)
                            last = mm(work[2 + c][:, cols], kc, qT[:, h, c * P:(c + 1) * P], start=True, stop=True)
                        last.then_inc(s_pe_kk, 1)
                elif kind == "tok":
                    pe.wait_ge(s_lt_done, 2 * (L + 1))
                    pe.wait_ge(s_qk_done, 2 * (L + 1))
                    pe.wait_ge(s_silu_done, 6 * (L + 1))
                    for c in range(TT):
                        for h, r, cols in heads(c):
                            tr(work[c][:, cols], kT[:, h, c * P:(c + 1) * P], ident)
                            last = tr(work[2 + c][:, cols], vT[:, h, c * P:(c + 1) * P], ident)
                        last.then_inc(s_pe_tok, 1)
                elif kind == "level" and i == 0:
                    pe.wait_ge(s_kd_done, 8 * (L + 1))
                    pe.wait_ge(s_vb_done, 8 * (L + 1))
                    for c in range(TT):
                        pe.wait_ge(s_xt_done, 2 * L + c + 1)
                        for h, r, cols in heads(c):
                            last = tr(work[2 * c][:, cols], xt[:, r, :], ident)
                        last.then_inc(s_pe_x0, 1)
                elif kind == "level":
                    for c in range(TT):
                        pe.wait_ge(s_pool_lts, 12 * L + 2 * (i - 1) + c + 1)
                        if i == 1:
                            pe.wait_ge(s_x0_sb, 2 * L + c + 1)
                        else:
                            pe.wait_ge(s_x_upd, 12 * L + 2 * (i - 2) + c + 1)
                        for h, r, cols in heads(c):
                            last = mm(work[2 * c][:, cols], lts[:, r, :], xi[:, r, :], start=True, stop=True)
                        last.then_inc(s_pe_t, 1)
                    for c in range(TT):
                        pe.wait_ge(s_t_sb, 12 * L + 2 * (i - 1) + c + 1)
                        for h, r, cols in heads(c):
                            if i < 6:
                                mm(work[2 * c][:, cols], xt[:, r, :], tt[:, r, :], start=True, stop=True)
                            last = mm(work[2 * c + 1][:, cols], tt[:, r, :], xt[:, r, :], start=True, stop=True)
                        last.then_inc(s_pe_dx, 1)
                elif kind == "scan":
                    pe.wait_ge(s_x_upd, 12 * (L + 1))
                    for h, r, cols in heads(0):
                        last = mm(work[0][:, cols], xt[:, h, :], vb[:, h, :], start=True, stop=True)
                    last.then_inc(s_pe_u0, 1)
                    for h, r, cols in heads(1):
                        last = mm(work[1][:, cols], kd[:, r, :], xt[:, r, :], start=True, stop=True)
                    last.then_inc(s_pe_w, 1)
                    pe.wait_ge(s_vn0_done, L + 1)
                    for h, r, cols in heads(0):
                        last = mm(work[2][:, cols], kd[:, h, :], vn0[:, h, :], start=True, stop=True)
                    last.then_inc(s_pe_s, 1)
                    pe.wait_ge(s_w_done, L + 1)
                    pe.wait_ge(s_s_done, L + 1)
                    for h, r, cols in heads(1):
                        mm(work[3][:, cols], xt[:, r, :], vb[:, r, :], start=True, stop=False)
                        last = mm(work[3][:, cols], w_sb[:, h, :], s_sb[:, h, :], start=False, stop=True)
                    last.then_inc(s_pe_u1, 1)
                    pe.wait_ge(s_vn1_done, L + 1)
                    pe.wait_ge(s_qdec_done, L + 1)
                    for h in range(HEADS):
                        o, a = work[h // 2], (h % 2) * T
                        mm(o[:, a:a + P], vn0[:, h, :], qk[:, h, :], start=True, stop=True)
                        mm(o[:, a + P:a + T], s_sb[:, h, :], qdec[:, h, :], start=True, stop=False)
                        last = mm(o[:, a + P:a + T], vn1[:, h, :], qk[:, 4 + h, :], start=False, stop=True)
                        if h % 2:
                            last.then_inc(s_pe_o, 1)
                elif kind in ("scnorm", "headnorm"):
                    for j, dst in enumerate((stat, turned) if kind == "scnorm" else (work[2], work[3])):
                        pe.wait_ge(s_sq_done, n["sq"] + j + 1)
                        mm(dst[:], ones, sq[:, j % 2, :], start=True, stop=True).then_inc(s_pe_stat, 1)
                elif kind == "flog":
                    pe.wait_ge(s_shifted, DT * (L + 1))
                    for c in range(TT):
                        for kt in range(DT):
                            last = mm(turned[:, c * 8:c * 8 + 8], hf[:, kt, c * P:(c + 1) * P],
                                      p2_(L, "w_f", kt * 8, kt * 8 + 8), start=(kt == 0), stop=(kt == DT - 1))
                    last.then_inc(s_pe_f, 1)
                elif kind == "forget":
                    pe.wait_ge(s_g_in, 4 * (L + 1))
                    pe.wait_ge(s_bu_sb, ST * (L + 1))
                    pe.wait_ge(s_lf_done, L + 1)
                    for j in range(AH // 2):
                        for e in range(2):
                            h = 2 * j + e
                            mm(work[j][:, e * T:(e + 1) * T], s2["lf"][:, h:h + 1].to_broadcast([P, P]), triu_ones,
                               start=True, stop=False, skip_group_check=True)
                            last = mm(work[j][:, e * T + P:(e + 1) * T], s2["lf"][:, 8 + h:9 + h].to_broadcast([P, P]),
                                      triu, start=False, stop=True, skip_group_check=True)
                        last.then_inc(s_pe_ck, 1)
                elif kind in ("ssm", "gelu"):
                    if kind == "ssm" and i == 0:
                        evacuated(pe, 2, L, "pair", 0)
                        evacuated(pe, 2, L, "pair", 1)
                        pe.wait_ge(s_cre_done, L + 1)
                    if kind == "ssm":
                        if ST * L + i - 1 > 0:
                            pe.wait_ge(s_bu_sb, ST * L + i - 1)
                        ut, q = i // 4, i % 4
                        rows = slice(32 * q, 32 * q + 32)
                        for e, name in enumerate(("b_re", "b_im")):
                            last = mm(work[i % 2][:, e * T:(e + 1) * T], p2_(L, name, ut * P, ut * P + P)[rows, :],
                                      u2[rows, ut, :], start=True, stop=True)
                        last.then_inc(s_pe_bu, 1)
                    for k in ([i - 2] if i >= 2 else []) if kind == "ssm" else [ST - 2, ST - 1]:
                        pe.wait_ge(s_s_sum, 2 * (ST * L + k + 1))
                        kt, kq = k // 4, k % 4
                        o = work[2 + kt // 2][32 * kq:32 * kq + 32, (kt % 2) * T:(kt % 2 + 1) * T]
                        mm(o, cp[:, 0, k, :], sst[:, k % 2, 0:T], start=True, stop=False, skip_group_check=True)
                        mm(o, cp[:, 1, k, :], sst[:, k % 2, T:2 * T], start=False, stop=True,
                           skip_group_check=True).then_inc(s_pe_y, 1)
                elif kind == "vtok":
                    pe.wait_ge(s_cm_done, 8 * (L + 1))
                    for c in range(TT):
                        for hp in range(4):
                            last = tr(work[c][:, hp * P:(hp + 1) * P], v2[:, hp, c * P:(c + 1) * P], ident)
                        last.then_inc(s_pe_vt, 1)
                elif kind == "head":
                    hp, e = i // 2, i % 2
                    rows = slice(64 * e, 64 * e + 64)
                    if i == 0:
                        pe.wait_ge(s_vt_sb, 2 * (L + 1))
                    if AH * L + i - 1 > 0:
                        pe.wait_ge(s_lg_done, AH * L + i - 1)
                    mm(work[i % 2][:, 0:T], q2[rows, hp, P:T], k2[rows, hp, :], start=True, stop=True)
                    mm(work[i % 2][:, T:T + P], q2[rows, hp, 0:P], k2[rows, hp, 0:P], start=True,
                       stop=True).then_inc(s_pe_sc, 1)
                    for k in ([i - 1] if i >= 1 else []) + ([i] if i == AH - 1 else []):
                        pe.wait_ge(s_p_norm, 2 * (AH * L + k + 1))
                        if AH * L + k > 0:
                            pe.wait_ge(s_pt_sb, AH * L + k)
                        if i == AH - 1 and k == i:
                            attend(L, k - 1, n["h"])
                        tr(turned[:, 0:P], pr[:, k % 2, T:T + P], ident)
                        tr(turned[:, P:T], pr[:, k % 2, 0:P], ident)
                        tr(turned[:, T:T + P], pr[:, k % 2, P:T], ident).then_inc(s_pe_pt, 1)
                        if k == i:
                            attend(L, k, n["h"])

        @block.scalar
        def _(act):
            f = nc.scalar.activation
            links = [0]

            def link(ins):
                links[0] += 1
                ins.then_inc(s_act_self, 1)
                act.wait_ge(s_act_self, links[0])

            fed = [0]

            def round_weights(limit):
                while fed[0] < min(limit, TOTAL["split"]):
                    v = fed[0]
                    if v % 2 == 0:
                        arrived(act, chunk_of_unit[v])
                    if v - SLOTS + 1 > 0:
                        act.wait_ge(s_unit_done, v - SLOTS + 1)
                    f(w_hi[:, v % SLOTS, :], raw[:, chunk_of_unit[v] % RAWS, (v % 2) * UNIT:(v % 2 + 1) * UNIT],
                      ACT.Copy).then_inc(s_hi_ready, 1)
                    fed[0] += 1

            def squares(n, sources, waits, count=4):
                for j in range(count):
                    waits(j)
                    if n + j - 1 > 0:
                        act.wait_ge(s_pe_stat, n + j - 1)
                    f(sq[:, j % 2, :], sources(j), ACT.Square).then_inc(s_sq_done, 1)

            def round_h(n, t, first=0, shift=None):
                act.wait_ge(s_hf_done, n["h"] + t - first + 1)
                if shift is None:
                    f(h_hi[:, t, :], hf[:, t, :], ACT.Copy).then_inc(s_hhi_done, 1)
                else:
                    f(h_hi[:, t, :], hf[:, t, :], ACT.Identity, bias=shift).then_inc(s_hhi_done, 1)

            def round_g(g, slot):
                act.wait_ge(s_hid_done, g + 1)
                f(g_hi[:, slot, :], hid[:, g % 2, :], ACT.Copy).then_inc(s_ghi_done, 1)

            def root(n):
                act.wait_ge(s_pe_stat, n["sq"] + 4)
                f(std[:], stat[:, 0:T], ACT.Sqrt, bias=EPS, scale=1.0 / D).then_inc(s_sqrt_done, 1)

            act.wait_ge(con_in, 16)
            f(csil[:, 0, :], c_("c"), ACT.Tanh, scale=0.5).then_inc(s_c_th, 1)
            act.wait_ge(x_ld, 16)
            act.wait_ge(p1_ld, 16)
            for B, L, kind, i, n in NUMBERED:
                bank = stream[n["pair"] % 2]
                units = UNITS_OF.get(kind, 0)
                free = banks[n["pair"] % 2]
                if units:
                    round_weights(n["split"] + units + 2)
                    if kind != "down":
                        act.wait_ge(s_unit_done, n["split"] + units)
                if kind in ("norm", "pre", "post", "final"):
                    if kind == "norm" and i == 1:
                        squares(n["sq"], lambda j: x[:, 2 * j:2 * j + 2, :], lambda j: evacuated(act, 1, L, "out", j))
                    elif kind == "post" and i == 1:
                        squares(n["sq"], lambda j: hf[:, 2 * j:2 * j + 2, :], lambda j: evacuated(act, 2, L, "mout", j))
                    elif kind == "post":
                        squares(n["sq"], lambda j: work[j][:], lambda j: act.wait_ge(s_unit_done, n["split"]))
                    else:
                        base = n["x"] - 4

                        def x_ready(j):
                            if base >= 0:
                                act.wait_ge(s_x_done, base + j + 1)
                        squares(n["sq"], lambda j: x[:, 2 * j:2 * j + 2, :], x_ready)
                    if n["split"] == 0:
                        round_weights(2)
                    root(n)
                    if kind in ("norm", "pre"):
                        if n["split"] > 0:
                            act.wait_ge(s_unit_done, n["split"])
                        for t in range(DT):
                            round_h(n, t, shift=modv[:, L, i, 0, t:t + 1] if B == 2 else None)
                elif kind == "crow":
                    for half, src in enumerate((turned, work[3])):
                        act.wait_ge(s_pe_crow, half + 1)
                        f(crow[:, 512 * half:512 * half + 512], src[:], ACT.Copy).then_inc(s_crow_done, 1)
                elif kind == "gates":
                    act.wait_ge(s_ba_ap, L + 1)
                    b_part = sm["ba"].rearrange("p (c n) -> p c n", c=2)[:, :, 0:4]
                    f(sm["tb"].rearrange("p (c n) -> p c n", c=2), b_part, ACT.Tanh, scale=0.5)
                    f(sm["ea"], p1_(L, "a_log"), ACT.Exp)
                    link(f(sm["ab"], sm["ap"], ACT.Abs))
                    link(f(sm["ab"], sm["ab"], ACT.Exp, scale=-1.0))
                    f(sm["ln"], sm["ab"], ACT.Ln, bias=1.0).then_inc(s_act_ap, 1)
                elif kind == "decay":
                    act.wait_ge(s_dd_done, L + 1)
                    f(sm["eg"], sm["gc"][:, 0:8], ACT.Exp)
                    f(sm["ekd"], sm["d"], ACT.Exp).then_inc(s_act_eg, 1)
                    act.wait_ge(s_pe_grow, 2 * (L + 1))
                    f(egr, work[3][:], ACT.Exp).then_inc(s_egr_done, 1)
                    for c in range(TT):
                        act.wait_ge(s_dpre, 8 * L + 4 * c + 4)
                        f(dec[:, 4 * c:4 * c + 4, :], dec[:, 4 * c:4 * c + 4, :], ACT.Exp).then_inc(s_dec_done, 1)
                elif kind == "pair" and B == 1 and i < 6:
                    if i >= 2:
                        act.wait_ge(s_conv_done, 12 * L + 2 * (i - 1))
                    elif L == 0:
                        act.wait_ge(s_pads, 1)
                    if 6 * L + i - 1 > 0:
                        act.wait_ge(s_silu_done, 6 * L + i - 1)
                    for e in range(2):
                        last_tap = (2 * i + e) * TAPS + TAPS - 1
                        f(yv[:, 2 * (i % 2) + e, :], bank[:, e, :], ACT.Copy,
                          scale=p1_(L, "conv", last_tap, last_tap + 1))
                    f(rawp[:, i % 2, :, 3:3 + T], bank[:], ACT.Copy).then_inc(free, 1)
                    act.wait_ge(s_conv_done, 12 * L + 2 * (i + 1))
                    f(th[:, 2 * (i % 2):2 * (i % 2) + 2, :], yv[:, 2 * (i % 2):2 * (i % 2) + 2, :], ACT.Tanh,
                      scale=0.5).then_inc(s_th_done, 1)
                elif kind == "pair" and B == 1 and i < 8:
                    f(zs[:, 2 * (i - 6):2 * (i - 6) + 2, :], bank[:], ACT.Tanh, scale=0.5).then_inc(s_z_th, 1)
                elif kind == "pair" and B == 1 and i < 12:
                    act.wait_ge(s_silu_done, 6 * (L + 1))
                    f(th[:, i - 8, :], bank[:, 0, :], ACT.Copy).then_inc(s_c_done, 1)
                elif kind == "qknorm":
                    round_weights(n["split"] + 4)
                    src = [qT[:, 0:2, :], qT[:, 2:4, :], kT[:, 0:2, :], kT[:, 2:4, :]]
                    squares(n["sq"], lambda j: src[j], lambda j: act.wait_ge(s_silu_done, 6 * L + j + 1))
                    for j in range(4):
                        act.wait_ge(s_pe_stat, n["sq"] + j + 1)
                        scale = float(HD) if j < 2 else 1.0
                        f(sd[j], work[j][:], ACT.Sqrt, scale=scale, bias=4 * EPS * scale).then_inc(s_qk_sqrt, 1)
                elif kind == "tok":
                    for c in range(TT):
                        act.wait_ge(s_pe_tok, 2 * L + c + 1)
                        for h in range(HEADS):
                            r = c * HEADS + h
                            by = sm["ekd"] if c == 0 else sm["bke"]
                            f(kd[:, r, :], work[c][:, h * P:(h + 1) * P], ACT.Copy, scale=by[:, r:r + 1])\
                                .then_inc(s_kd_done, 1)
                elif kind == "level":
                    for c in range(TT):
                        if i == 0:
                            act.wait_ge(s_qdec_done, L + 1)
                            act.wait_ge(s_pe_x0, 2 * L + c + 1)
                            f(xi[:, 4 * c:4 * c + 4, :], work[2 * c][:], ACT.Copy).then_inc(s_x0_sb, 1)
                        else:
                            act.wait_ge(s_pe_t, 12 * L + 2 * (i - 1) + c + 1)
                            f(tt[:, 4 * c:4 * c + 4, :], work[2 * c][:], ACT.Copy).then_inc(s_t_sb, 1)
                elif kind == "scan":
                    for src, got, dst, k, done in ((0, s_pe_u0, vn0, 1.0, s_vn0_done), (1, s_pe_w, w_sb, -1.0, s_w_done),
                                                   (2, s_pe_s, s_sb, 1.0, s_s_done), (3, s_pe_u1, vn1, 1.0, s_vn1_done)):
                        act.wait_ge(got, L + 1)
                        f(dst, work[src][:], ACT.Copy, scale=k).then_inc(done, 1)
                elif kind == "scnorm":
                    squares(n["sq"], lambda j: sc[:, 2 * j:2 * j + 2, :],
                            lambda j: evacuated(act, 1, L, "pair", 12 + j), count=2)
                    for j, b in enumerate((stat, turned)):
                        act.wait_ge(s_pe_stat, n["sq"] + j + 1)
                        f(scd[j], b[:], ACT.Sqrt, scale=1.0 / HD, bias=EPS).then_inc(s_os_sqrt, 1)
                    act.wait_ge(s_unit_done, n["split"])
                elif kind == "headnorm":
                    for t in range(4, DT):
                        round_h(n, t, first=8)
                    squares(n["sq"], lambda j: work[j][:], lambda j: act.wait_ge(s_pe_o, 2 * L + j + 1), count=2)
                    for j, b in enumerate((work[2], work[3])):
                        act.wait_ge(s_pe_stat, n["sq"] + j + 1)
                        f(sd[j], b[:], ACT.Sqrt, scale=4.0 / HD, bias=4.0 * EPS).then_inc(s_os_sqrt, 1)
                    for t in range(4):
                        round_h(n, t)
                elif kind == "gu":
                    if n["g"] - 1 > 0:
                        act.wait_ge(s_hid_done, n["g"] - 1)
                    f(gate_t[:, n["g"] % 2, :], bank[:, 0, :], ACT.Tanh, scale=0.5).then_inc(s_gate_th, 1)
                    round_g(n["g"], i % 4)
                elif kind == "coef" and i == 0:
                    t = s2
                    act.wait_ge(p2_ld, 16 * (L + 1))
                    f(t["dt"], p2_(L, "log_dt"), ACT.Exp).then_inc(s_dt_done, 1)
                elif kind == "coef" and i == 2:
                    act.wait_ge(s_co_dve, 2 * (L + 1))
                    f(t["ta"], t["re"], ACT.Tanh, scale=0.5)
                    f(t["sh"], t["ph"], ACT.Sin, scale=3.1415925)
                    f(t["sn"], t["ph"], ACT.Sin, scale=6.2831850).then_inc(s_co_act, 1)
                elif kind == "pair" and B == 2 and i < 8:
                    dst = (u2, q2, k2, v2)[i // 2]
                    f(dst[:, 2 * (i % 2):2 * (i % 2) + 2, :], bank[:], ACT.Copy).then_inc(free, 1)
                elif kind == "pair" and B == 2:
                    dst, t = (sga, i - 8) if i < 12 else (sgb, i - 12)
                    f(dst[:, 2 * t:2 * t + 2, :], bank[:], ACT.Tanh, scale=0.5).then_inc(free, 1)
                elif kind == "ssm":
                    act.wait_ge(s_tab_frac, ST * L + i + 1)
                    if 2 * (ST * L + i - 1) > 0:
                        act.wait_ge(s_s_sum, 2 * (ST * L + i - 1))
                    f(tab[:, i % 2, 0:512], Bx["arg"], ACT.Sin, scale=6.2831850)
                    f(tab[:, i % 2, 512:768], Bx["arg"][:, 0:256], ACT.Sin, scale=6.2831850).then_inc(s_tab_sin, 1)
                    act.wait_ge(s_pe_bu, ST * L + i + 1)
                    if 2 * (ST * L + i - 1) > 0:
                        act.wait_ge(s_z_in, 2 * (ST * L + i - 1))
                    f(bu[:, i % 2, :], work[i % 2][:], ACT.Copy).then_inc(s_bu_sb, 1)
                elif kind == "gelu":
                    act.wait_ge(s_g_in, 4 * (L + 1))
                    f(G[:, 1, :], G[:, 1, :], ACT.Tanh, scale=0.7978845608028654).then_inc(s_g_tanh, 1)
                    for t in range(4):
                        round_g(n["g"] + t, t)
                elif kind == "flog":
                    act.wait_ge(s_f_dve, L + 1)
                    link(f(s2["ab"], s2["f"], ACT.Abs))
                    link(f(s2["ab"], s2["ab"], ACT.Exp, scale=-1.0))
                    f(s2["ln"], s2["ab"], ACT.Ln, bias=1.0).then_inc(s_f_act, 1)
                elif kind == "vtok":
                    for c in range(TT):
                        act.wait_ge(s_pe_vt, 2 * L + c + 1)
                        f(vt[:, c, :], work[c][:], ACT.Copy).then_inc(s_vt_sb, 1)
                elif kind == "head":
                    if AH * L + i - 1 > 0:
                        act.wait_ge(s_pe_pt, AH * L + i - 1)
                    for e, cols in enumerate((slice(0, T), slice(T, T + P))):
                        k = 2 * i + e
                        act.wait_ge(s_nm_done, 2 * AH * L + k + 1)
                        f(pr[:, i % 2, cols], lg[:, i % 2, cols], ACT.Exp, bias=s2["mxn"][:, k:k + 1],
                          accum_out=s2["sum"][:, k:k + 1]).then_inc(s_p_exp, 1)
                    for k in ([i - 1] if i >= 1 else []) + ([i] if i == AH - 1 else []):
                        act.wait_ge(s_pe_pt, AH * L + k + 1)
                        if AH * L + k - 1 > 0:
                            act.wait_ge(s_pe_at, AH * L + k - 1)
                        f(pt[:, k % 2, :], turned[:, 0:384], ACT.Copy).then_inc(s_pt_sb, 1)
                    if i == AH - 1:
                        act.wait_ge(s_unit_done, AT[2, L, "glu", 0]["split"])
                        for t in range(4):
                            round_h(n, t)
                elif kind == "glu":
                    if DT * L + i - 1 > 0:
                        act.wait_ge(s_glu_done, DT * L + i - 1)
                    f(gate_t[:, i % 2, :], bank[:, 1, :], ACT.Tanh, scale=0.5).then_inc(s_gate_th, 1)
                elif kind == "aout":
                    for t in ((4, 5), (6, 7), (), (0, 1, 2, 3))[i]:
                        round_h(n, t, first=2 * ((i + 2) % 4) if i < 2 else 2)

        @block.vector
        def _(dve):
            v = nc.vector
            links = [0]

            def link(ins):
                links[0] += 1
                ins.then_inc(s_dve_self, 1)
                dve.wait_ge(s_dve_self, links[0])

            fed = [0]

            def low_weights(limit):
                while fed[0] < min(limit, TOTAL["split"]):
                    q = fed[0]
                    dve.wait_ge(s_hi_ready, q + 1)
                    v.tensor_tensor(w_lo[:, q % SLOTS, :],
                                    raw[:, chunk_of_unit[q] % RAWS, (q % 2) * UNIT:(q % 2 + 1) * UNIT],
                                    w_hi[:, q % SLOTS, :].bitcast(F32), ALU.subtract).then_inc(s_lo_ready, 1)
                    fed[0] += 1

            def low_h(n, t, first=0, shift=None):
                dve.wait_ge(s_hhi_done, n["h"] + t - first + 1)
                if shift is None:
                    v.tensor_tensor(h_lo[:, t, :], hf[:, t, :], h_hi[:, t, :].bitcast(F32), ALU.subtract)\
                        .then_inc(s_hlo_done, 1)
                else:
                    v.scalar_tensor_tensor(h_lo[:, t, :], hf[:, t, :], shift, h_hi[:, t, :].bitcast(F32), ALU.add,
                                           ALU.subtract).then_inc(s_hlo_done, 1)

            def inverse_root():
                link(v.reciprocal(rstd[:], std[:]))

            def turns(i, k):
                if k > 0:
                    dve.wait_ge(s_tab_sin, k)
                for e in range(2):
                    ins = v.tensor_scalar(Bx["arg"][:, e * T:(e + 1) * T], c_("time"), s2["ph"][:, i:i + 1], 0.25 * e,
                                          ALU.mult, ALU.add)
                link(ins)
                v.tensor_scalar(Bx["rnd"], Bx["arg"], ROUND, ROUND, ALU.add, ALU.subtract).then_inc(s_tab_arg, 1)

            link(v.memset(rawp[:, :, :, 0:3], 0.0))
            v.memset(scp[:, :, 0:2], 0.0).then_inc(s_pads, 1)
            dve.wait_ge(s_c_th, 1)
            dve.wait_ge(con_in, 16)
            link(v.scalar_tensor_tensor(csil[:, 0, :], csil[:, 0, :], 1.0, c_("c"), ALU.add, ALU.mult))
            v.tensor_scalar(csil[:, 1, :], csil[:, 0, :], 0.5, None, ALU.mult).then_inc(s_csil_done, 1)
            dve.wait_ge(x_ld, 16)
            dve.wait_ge(p1_ld, 16)
            for B, L, kind, i, n in NUMBERED:
                bank = stream[n["pair"] % 2]
                units = UNITS_OF.get(kind, 0)
                free = banks[n["pair"] % 2]
                if units:
                    low_weights(n["split"] + units + 2)
                    if kind != "down":
                        dve.wait_ge(s_unit_done, n["split"] + units)
                if kind in ("norm", "pre"):
                    if n["split"] == 0:
                        low_weights(2)
                    dve.wait_ge(s_sqrt_done, n["norm"] + 1)
                    inverse_root()
                    gain = p1_(L, f"norm{i + 1}") if B == 1 else s2["A"][:, 8 * i:8 * i + 8]
                    for t in range(DT + 2):
                        if t < DT:
                            v.scalar_tensor_tensor(hf[:, t, :], x[:, t, :], gain[:, t:t + 1], rstd[:], ALU.mult,
                                                   ALU.mult).then_inc(s_hf_done, 1)
                        if t >= 2:
                            low_h(n, t - 2, shift=modv[:, L, i, 0, t - 2:t - 1] if B == 2 else None)
                    if (B, kind, i) == (2, "pre", 1):
                        for t in range(DT):
                            v.tensor_scalar(hf[:, t, :], hf[:, t, :], modv[:, L, i, 0, t:t + 1], None, ALU.add)\
                                .then_inc(s_shifted, 1)
                elif kind == "final":
                    dve.wait_ge(s_sqrt_done, n["norm"] + 1)
                    inverse_root()
                    for t in range(DT):
                        v.scalar_tensor_tensor(x[:, t, :], x[:, t, :], c_("final", t, t + 1), rstd[:], ALU.mult, ALU.mult)\
                            .then_inc(s_x_done, 1)
                elif kind == "post":
                    dve.wait_ge(s_sqrt_done, n["norm"] + 1)
                    inverse_root()
                    for j in range(5):
                        for t in ((2 * j, 2 * j + 1) if j < 4 else ()):
                            y = hf[:, t, :] if i == 1 else work[j][:, (t % 2) * T:(t % 2 + 1) * T]
                            v.scalar_tensor_tensor(hf[:, t, :], y, s2["B"][:, 8 * i + t:8 * i + t + 1], rstd[:],
                                                   ALU.mult, ALU.mult).then_inc(s_y_scaled, 1)
                        if j:
                            dve.wait_ge(s_y_scaled, n["y"] + 2 * j)
                            two = x[:, 2 * j - 2:2 * j, :]
                            v.tensor_tensor(two, two, hf[:, 2 * j - 2:2 * j, :], ALU.add).then_inc(s_x_done, 1)
                elif kind == "acc":
                    dve.wait_ge(s_unit_done, n["split"])
                    for j in range(4):
                        v.tensor_tensor(x[:, 2 * j:2 * j + 2, :], x[:, 2 * j:2 * j + 2, :],
                                        work[j][:].rearrange("p (n t) -> p n t", t=T), ALU.add).then_inc(s_x_done, 1)
                elif kind == "mod":
                    chunk = chunk_of_mod[n["mod"]]
                    arrived(dve, chunk)
                    dve.wait_ge(s_crow_done, 2)
                    for e in range(2):
                        rows = raw[:, chunk % RAWS, e * UNIT:(e + 1) * UNIT]
                        v.tensor_tensor_reduce(rows, rows, crow[:], 1.0, 0.0, ALU.mult, ALU.add,
                                               modacc[:, 2 * i + e:2 * i + e + 1]).then_inc(s_mod_used, 1)
                elif kind == "modsum":
                    dve.wait_ge(s_mod_used, 2 * n["mod"])
                    v.tensor_tensor(modv[:, B - 1].rearrange("p a b c -> p (a b c)"), modacc[:],
                                    p1_(B - 1, "mod_b"), ALU.add).then_inc(s_mod_sb, 1)
                elif kind == "gates":
                    dve.wait_ge(s_pe_ba, L + 1)
                    link(v.tensor_copy(sm["ba"], work[0][:, 0:16]))
                    ba = sm["ba"].rearrange("p (c n) -> p c n", c=2)
                    v.tensor_tensor(sm["ap"].rearrange("p (c n) -> p c n", c=2), ba[:, :, 4:8],
                                    p1_(L, "dt_bias").unsqueeze(1).to_broadcast([P, 2, 4]), ALU.add)\
                        .then_inc(s_ba_ap, 1)
                    dve.wait_ge(s_act_ap, L + 1)
                    v.tensor_scalar(sm["beta"], sm["tb"], 0.5, 0.5, ALU.mult, ALU.add)
                    v.tensor_scalar(sm["hb"], sm["tb"], 0.25, 0.25, ALU.mult, ALU.add)
                    link(v.scalar_tensor_tensor(sm["sp"], sm["ap"], 0.0, sm["ln"], ALU.max, ALU.add))
                    v.scalar_tensor_tensor(sm["g"].rearrange("p (c n) -> p c n", c=2),
                                           sm["sp"].rearrange("p (c n) -> p c n", c=2), -1.0,
                                           sm["ea"].unsqueeze(1).to_broadcast([P, 2, 4]), ALU.mult, ALU.mult)\
                        .then_inc(s_gates_done, 1)
                elif kind == "decay":
                    dve.wait_ge(s_pe_gc, L + 1)
                    v.tensor_copy(sm["gc"], work[1][:, 0:16]).then_inc(s_gc_sb, 1)
                    dve.wait_ge(s_gc_sb, L + 1)
                    v.tensor_tensor(sm["d"], sm["gc"][:, 8:16], sm["gc"][:, 0:8], ALU.subtract).then_inc(s_dd_done, 1)
                    for c in range(TT):
                        dve.wait_ge(s_pe_grow, 2 * L + c + 1)
                        if c == 1:
                            dve.wait_ge(s_egr_done, L + 1)
                        for h in range(HEADS):
                            r = c * HEADS + h
                            v.tensor_scalar(dec[:, r, :], work[2 + c][:, h * P:(h + 1) * P], sm["gc"][:, r:r + 1], 0.0,
                                            ALU.subtract, ALU.min).then_inc(s_dpre, 1)
                    dve.wait_ge(s_act_eg, L + 1)
                    link(v.tensor_tensor(sm["bke"], sm["beta"], sm["eg"], ALU.mult))
                elif kind == "brow":
                    for c in range(TT):
                        dve.wait_ge(s_decm_done, 2 * L + c + 1)
                        dve.wait_ge(s_pe_brow, 2 * L + c + 1)
                        v.tensor_tensor(A["lt"][:, 512 * c:512 * c + 512], A["dec"][:, 512 * c:512 * c + 512], work[c][:],
                                        ALU.mult).then_inc(s_lt_half, 1)
                elif kind == "pair" and B == 1 and i < 6:
                    evacuated(dve, B, L, kind, i)
                    if L == 0 and i == 0:
                        dve.wait_ge(s_pads, 1)
                    for k in range(TAPS - 1):
                        for e in range(2):
                            tile = 2 * i + e
                            y = yv[:, 2 * (i % 2) + e, :]
                            src = rawp[:, i % 2, e, k:k + T]
                            tap = p1_(L, "conv", tile * TAPS + k, tile * TAPS + k + 1)
                            ins = v.scalar_tensor_tensor(y, src, tap, y, ALU.mult, ALU.add)
                            if k == TAPS - 2:
                                ins.then_inc(s_conv_done, 1)
                            elif e == 1:
                                link(ins)
                    dve.wait_ge(s_th_done, 6 * L + i + 1)
                    dst = (qT, kT, vT)[i // 2]
                    v.scalar_tensor_tensor(dst[:, 2 * (i % 2):2 * (i % 2) + 2, :], th[:, 2 * (i % 2):2 * (i % 2) + 2, :],
                                           1.0, yv[:, 2 * (i % 2):2 * (i % 2) + 2, :], ALU.add, ALU.mult)\
                        .then_inc(s_silu_done, 1)
                elif kind == "pair" and B == 1 and i < 8:
                    t = 2 * (i - 6)
                    dve.wait_ge(s_z_th, 2 * L + i - 5)
                    v.scalar_tensor_tensor(zs[:, t:t + 2, :], zs[:, t:t + 2, :], 1.0, bank[:], ALU.add, ALU.mult)\
                        .then_inc(free, 1)
                elif kind == "pair" and B == 1 and i < 12:
                    t = i - 8
                    dve.wait_ge(s_c_done, 4 * L + t + 1)
                    v.tensor_tensor(scp[:, t, 2:2 + T], th[:, t, :], bank[:, 1, :], ALU.mult).then_inc(free, 1)
                    evacuated(dve, B, L, kind, i)
                    for k in range(STAPS):
                        tap = p1_(L, "sconv", t * STAPS + k, t * STAPS + k + 1)
                        src = scp[:, t, k:k + T]
                        if k == 0:
                            link(v.tensor_scalar(sc[:, t, :], src, tap, None, ALU.mult))
                        else:
                            link(v.scalar_tensor_tensor(sc[:, t, :], src, tap, sc[:, t, :], ALU.mult, ALU.add))
                elif kind == "pair" and B == 1:
                    t = 2 * (i - 12)
                    v.tensor_tensor(sc[:, t:t + 2, :], sc[:, t:t + 2, :], bank[:], ALU.mult).then_inc(free, 1)
                elif kind == "qknorm":
                    low_weights(n["split"] + 4)
                    for j in range(4):
                        dve.wait_ge(s_qk_sqrt, 4 * L + j + 1)
                        link(v.reciprocal(sd[j], sd[j]))
                        dst = (qT, kT)[j // 2][:, 2 * (j % 2):2 * (j % 2) + 2, :]
                        v.tensor_tensor(dst, dst, sd[j].rearrange("p (n t) -> p n t", t=T), ALU.mult)\
                            .then_inc(s_qk_ready, 1)
                elif kind == "kk":
                    for c in range(TT):
                        dve.wait_ge(s_pe_kk, 2 * L + c + 1)
                        dve.wait_ge(s_lt_half, 2 * L + c + 1)
                        half = slice(512 * c, 512 * c + 512)
                        four = slice(4 * c, 4 * c + 4)
                        v.tensor_tensor(A["lt"][:, half], A["lt"][:, half], work[c][:], ALU.mult)\
                            .then_inc(s_lt_done, 1)
                        v.tensor_tensor(A["qk"][:, half], A["dec"][:, half], work[2 + c][:], ALU.mult)\
                            .then_inc(s_qk_done, 1)
                        dve.wait_ge(s_lt_done, 2 * L + c + 1)
                        link(v.tensor_tensor(xt[:, four, :], lt[:, four, :],
                                             c_("m", 0, P).unsqueeze(1).to_broadcast([P, 4, P]), ALU.mult))
                        v.scalar_tensor_tensor(xt[:, four, :], xt[:, four, :], -1.0,
                                               ident.unsqueeze(1).to_broadcast([P, 4, P]), ALU.mult, ALU.add)\
                            .then_inc(s_xt_done, 1)
                elif kind == "tok":
                    dve.wait_ge(s_pe_tok, 2 * (L + 1))
                    for c in range(TT):
                        for h in range(HEADS):
                            r = c * HEADS + h
                            v.tensor_scalar(vb[:, r, :], work[2 + c][:, h * P:(h + 1) * P], sm["hb"][:, r:r + 1], None,
                                            ALU.mult).then_inc(s_vb_done, 1)
                elif kind == "level" and i:
                    for c in range(TT):
                        dve.wait_ge(s_pe_dx, 12 * L + 2 * (i - 1) + c + 1)
                        half = slice(512 * c, 512 * c + 512)
                        if i < 6:
                            v.tensor_tensor(A["x"][:, half], A["x"][:, half], work[2 * c][:], ALU.subtract)
                        v.tensor_tensor(A["xt"][:, half], A["xt"][:, half], work[2 * c + 1][:], ALU.subtract)\
                            .then_inc(s_x_upd, 1)
                elif kind == "scnorm":
                    for j in range(2):
                        dve.wait_ge(s_os_sqrt, 4 * L + j + 1)
                        link(v.reciprocal(scd[j], scd[j]))
                        for e in range(2):
                            t = 2 * j + e
                            v.scalar_tensor_tensor(hf[:, 4 + t, :], sc[:, t, :], p1_(L, "sc_g", t, t + 1),
                                                   scd[j][:, e * T:(e + 1) * T], ALU.mult, ALU.mult)\
                                .then_inc(s_hf_done, 1)
                elif kind == "headnorm":
                    for t in range(4, DT):
                        low_h(n, t, first=8)
                    for j in range(2):
                        dve.wait_ge(s_pe_o, 2 * L + j + 1)
                        dve.wait_ge(s_sq_done, n["sq"] + j + 1)
                        two = hf[:, 2 * j:2 * j + 2, :]
                        v.scalar_tensor_tensor(two, work[j][:].rearrange("p (n t) -> p n t", t=T), p1_(L, "dn_g"),
                                               zs[:, 2 * j:2 * j + 2, :], ALU.mult, ALU.mult)
                    for j in range(2):
                        dve.wait_ge(s_os_sqrt, 4 * L + j + 3)
                        link(v.reciprocal(sd[j], sd[j]))
                        two = hf[:, 2 * j:2 * j + 2, :]
                        v.tensor_tensor(two, two, sd[j].rearrange("p (n t) -> p n t", t=T), ALU.mult)\
                            .then_inc(s_hf_done, 2)
                        if j:
                            low_h(n, 0)
                            low_h(n, 1)
                    low_h(n, 2)
                    low_h(n, 3)
                elif kind == "out":
                    v.tensor_tensor(x[:, 2 * i:2 * i + 2, :], x[:, 2 * i:2 * i + 2, :], bank[:], ALU.add)\
                        .then_inc(free, 1)
                elif kind == "gu":
                    g = n["g"]
                    if g - 1 > 0:
                        dve.wait_ge(s_glo_done, g - 1)
                    dve.wait_ge(s_gate_th, n["gt"] + 1)
                    link(v.scalar_tensor_tensor(gate_t[:, g % 2, :], gate_t[:, g % 2, :], 1.0, bank[:, 0, :], ALU.add,
                                                ALU.mult))
                    v.scalar_tensor_tensor(hid[:, g % 2, :], gate_t[:, g % 2, :], 0.5, bank[:, 1, :], ALU.mult,
                                           ALU.mult).then_inc(s_hid_done, 1)
                    dve.wait_ge(s_hid_done, g + 1)
                    v.sem_inc(free, 1)
                elif kind == "mods":
                    dve.wait_ge(p2_ld, 16 * (L + 1))
                    dve.wait_ge(s_mod_sb, L + 1)
                    for sub in range(3):
                        eight = slice(8 * sub, 8 * sub + 8)
                        v.scalar_tensor_tensor(s2["A"][:, eight], modv[:, L, sub, 1, :], 1.0,
                                               p2_(L, "pre")[:, eight], ALU.add, ALU.mult)
                        link(v.scalar_tensor_tensor(s2["B"][:, eight], modv[:, L, sub, 2, :], 1.0 if sub == 1 else 0.5,
                                                    p2_(L, "post")[:, eight], ALU.mult, ALU.mult))
                elif kind == "coef" and i == 0:
                    t = s2
                    TS, TTn, STT = v.tensor_scalar, v.tensor_tensor, v.scalar_tensor_tensor
                    dve.wait_ge(s_dt_done, L + 1)
                    link(TS(t["re"], p2_(L, "a_re"), -1e-4, None, ALU.min))
                    link(TTn(t["im"], p2_(L, "a_im"), t["dt"], ALU.mult))
                    link(TTn(t["l2"], t["re"], t["re"], ALU.mult))
                    link(TTn(t["t1"], p2_(L, "a_im"), p2_(L, "a_im"), ALU.mult))
                    link(TTn(t["l2"], t["l2"], t["t1"], ALU.add))
                    link(v.reciprocal(t["l2"], t["l2"]))
                    link(TTn(t["t2"], t["re"], t["l2"], ALU.mult))
                    link(STT(t["den"], p2_(L, "a_im"), -1.0, t["l2"], ALU.mult, ALU.mult))
                elif kind == "coef" and i == 1:
                    TTn(t["re"], t["re"], t["dt"], ALU.mult).then_inc(s_co_dve, 1)
                    link(TS(t["ph"], t["im"], 0.15915494309189535, None, ALU.mult))
                    link(TS(t["t1"], t["ph"], ROUND, ROUND, ALU.add, ALU.subtract))
                    TTn(t["ph"], t["ph"], t["t1"], ALU.subtract).then_inc(s_co_dve, 1)
                elif kind == "coef" and i == 2:
                    dve.wait_ge(s_co_act, L + 1)
                    link(TS(t["t1"], t["ta"], -1.0, 1.0, ALU.mult, ALU.add))
                    link(v.reciprocal(t["t1"], t["t1"]))
                    link(STT(t["em"], t["ta"], 2.0, t["t1"], ALU.mult, ALU.mult))
                    link(TS(t["r"], t["em"], 1.0, None, ALU.add))
                    link(TTn(t["cs"], t["sh"], t["sh"], ALU.mult))
                    link(TS(t["cs"], t["cs"], -2.0, None, ALU.mult))
                elif kind == "coef" and i == 3:
                    link(TTn(t["t1"], t["em"], t["cs"], ALU.mult))
                    link(TTn(t["t1"], t["t1"], t["em"], ALU.add))
                    link(TTn(t["t1"], t["t1"], t["cs"], ALU.add))
                    link(TTn(t["sn"], t["sn"], t["r"], ALU.mult))
                    link(TTn(t["kr"], t["t1"], t["t2"], ALU.mult))
                    link(TTn(t["ki"], t["sn"], t["den"], ALU.mult))
                    link(TTn(t["kr"], t["kr"], t["ki"], ALU.subtract))
                    link(TTn(t["ki"], t["t1"], t["den"], ALU.mult))
                    link(TTn(t["sn"], t["sn"], t["t2"], ALU.mult))
                    link(TTn(t["ki"], t["ki"], t["sn"], ALU.add))
                elif kind == "coef" and i == 4:
                    wide = lambda a: a.unsqueeze(2).to_broadcast([P, ST, 32])
                    cre, cim = (p2_(L, k).rearrange("p (s n) -> p s n", n=32) for k in ("c_re", "c_im"))
                    tmp = Bx["pa"].rearrange("p (s n) -> p s n", n=32)
                    link(TTn(cp[:, 0], cre, wide(t["kr"]), ALU.mult))
                    link(TTn(tmp, cim, wide(t["ki"]), ALU.mult))
                    link(TTn(cp[:, 0], cp[:, 0], tmp, ALU.subtract))
                    link(TTn(cp[:, 1], cre, wide(t["ki"]), ALU.mult))
                    link(TTn(tmp, cim, wide(t["kr"]), ALU.mult))
                    STT(Bx["cp"][:, 512:1024], Bx["cp"][:, 512:1024], -1.0, Bx["pa"], ALU.mult, ALU.subtract)\
                        .then_inc(s_cre_done, 1)
                    dve.wait_ge(s_cre_done, L + 1)
                elif kind == "pair" and B == 2 and i >= 8:
                    evacuated(dve, B, L, kind, i)
                    dst, t = (sga, i - 8) if i < 12 else (sgb, i - 12)
                    two = dst[:, 2 * t:2 * t + 2, :]
                    link(v.tensor_scalar(two, two, 0.5, 0.5, ALU.mult, ALU.add))
                elif kind == "ssm":
                    k = ST * L + i
                    r = s2["r"][:, i:i + 1]
                    if i == 0:
                        turns(0, k)
                    dve.wait_ge(s_tab_sin, k + 1)
                    dve.wait_ge(s_bu_sb, k + 1)
                    v.tensor_tensor(Bx["pa"], tab[:, i % 2, 256:768], bu[:, i % 2, :], ALU.mult)\
                        .then_inc(s_z_in, 1)
                    v.tensor_tensor(Bx["pb"], tab[:, i % 2, 0:512], bu[:, i % 2, :], ALU.mult)\
                        .then_inc(s_z_in, 1)
                    if i + 1 < ST:
                        turns(i + 1, k + 1)
                    dve.wait_ge(s_z_in, 2 * (k + 1))
                    v.tensor_tensor(Bx["z"][:, 0:T], Bx["pa"][:, 0:T], Bx["pa"][:, T:2 * T], ALU.add)
                    link(v.tensor_tensor(Bx["z"][:, T:2 * T], Bx["pb"][:, T:2 * T], Bx["pb"][:, 0:T], ALU.subtract))
                    if 2 * (k - 1) > 0:
                        dve.wait_ge(s_s_sum, 2 * (k - 1))
                    for e in range(2):
                        v.tensor_tensor_scan(wv[:, i % 2, e * T:(e + 1) * T], r.to_broadcast([P, T]),
                                             Bx["z"][:, e * T:(e + 1) * T], 0.0, ALU.mult, ALU.add)\
                            .then_inc(s_wv_done, 1)
                elif kind == "gelu":
                    dve.wait_ge(s_pe_y, ST * (L + 1))
                    dve.wait_ge(s_s_sum, 2 * ST * (L + 1))
                    for t in range(4):
                        link(v.scalar_tensor_tensor(G[:, 0, t * T:(t + 1) * T], u2[:, t, :], p2_(L, "d", t, t + 1),
                                                    work[2 + t // 2][:, (t % 2) * T:(t % 2 + 1) * T], ALU.mult, ALU.add))
                    v.tensor_scalar(G[:, 2, :], G[:, 0, :], 0.5, None, ALU.mult).then_inc(s_g_in, 1)
                    link(v.tensor_tensor(G[:, 1, :], G[:, 0, :], G[:, 0, :], ALU.mult))
                    v.tensor_scalar(G[:, 1, :], G[:, 1, :], 0.044715, 1.0, ALU.mult, ALU.add).then_inc(s_g_in, 1)
                    dve.wait_ge(s_g_in, 4 * L + 2)
                    v.tensor_tensor(G[:, 1, :], G[:, 1, :], G[:, 0, :], ALU.mult).then_inc(s_g_in, 2)
                    dve.wait_ge(s_g_tanh, L + 1)
                    for t in range(4):
                        g = n["g"] + t
                        dve.wait_ge(s_glo_done, g - 1)
                        v.scalar_tensor_tensor(hid[:, g % 2, :], G[:, 1, t * T:(t + 1) * T], 1.0,
                                               G[:, 2, t * T:(t + 1) * T], ALU.add, ALU.mult).then_inc(s_hid_done, 1)
                elif kind == "flog":
                    dve.wait_ge(s_pe_f, L + 1)
                    v.tensor_tensor(s2["f"].rearrange("p (c n) -> p c n", c=2),
                                    turned[:, 0:16].rearrange("p (c n) -> p c n", c=2),
                                    p2_(L, "f_b").unsqueeze(1).to_broadcast([P, 2, 8]), ALU.add).then_inc(s_f_dve, 1)
                    dve.wait_ge(s_f_act, L + 1)
                    v.scalar_tensor_tensor(s2["lf"], s2["f"], 0.0, s2["ln"], ALU.min, ALU.subtract)\
                        .then_inc(s_lf_done, 1)
                elif kind == "forget":
                    for j in range(AH // 2):
                        dve.wait_ge(s_pe_ck, 4 * L + j + 1)
                        if j == 0:
                            dve.wait_ge(s_hid_done, n["g"])
                        src = work[j][:].rearrange("p (h n) -> p h n", h=2)
                        for cols, sc_ in ((slice(0, T), slice(0, T)), (slice(T, T + P), slice(0, P))):
                            w_ = cols.stop - cols.start
                            v.tensor_tensor(cm[:, 2 * j:2 * j + 2, cols], src[:, :, sc_],
                                            c_("pen")[:, cols].unsqueeze(1).to_broadcast([P, 2, w_]), ALU.add)\
                                .then_inc(s_cm_done, 1)
                elif kind == "head":
                    dve.wait_ge(s_pe_sc, AH * L + i + 1)
                    if i == 0:
                        dve.wait_ge(s_cm_done, 8 * (L + 1))
                    v.scalar_tensor_tensor(lg[:, i % 2, :], work[i % 2][:, 0:384], float(AD) ** -0.5, cm[:, i, :],
                                           ALU.mult, ALU.subtract).then_inc(s_lg_done, 1)
                    dve.wait_ge(s_lg_done, AH * L + i + 1)
                    for e, cols in enumerate((slice(0, T), slice(T, T + P))):
                        v.tensor_reduce(s2["mxn"][:, 2 * i + e:2 * i + e + 1], lg[:, i % 2, cols], AX.X, ALU.max,
                                        negate=True).then_inc(s_nm_done, 1)
                    for k in ([i - 1] if i >= 1 else []) + ([i] if i == AH - 1 else []):
                        dve.wait_ge(s_p_exp, 2 * (AH * L + k + 1))
                        link(v.reciprocal(s2["rec"][:, 2 * k:2 * k + 2], s2["sum"][:, 2 * k:2 * k + 2]))
                        for e, cols in enumerate((slice(0, T), slice(T, T + P))):
                            v.tensor_scalar(pr[:, k % 2, cols], pr[:, k % 2, cols], s2["rec"][:, 2 * k + e:2 * k + e + 1],
                                            None, ALU.mult).then_inc(s_p_norm, 1)
                    for kp in {3: [0], 5: [1], 7: [2, 3]}.get(i, []):
                        dve.wait_ge(s_pe_at, AH * L + 2 * kp + 2)
                        v.tensor_copy(hf[:, kp, :], work[2 + kp % 2][:, 0:T]).then_inc(s_hf_done, 1)
                    if i == AH - 1:
                        for t in range(4):
                            low_h(n, t)
                elif kind == "glu":
                    gt = gate_t[:, i % 2, :]
                    dve.wait_ge(s_gate_th, n["gt"] + 1)
                    v.scalar_tensor_tensor(gt, gt, 1.0, bank[:, 0, :], ALU.add, ALU.mult).then_inc(free, 1)
                    evacuated(dve, B, L, kind, i)
                    v.scalar_tensor_tensor(sga[:, i, :], gt, 0.5, sga[:, i, :], ALU.mult, ALU.mult)\
                        .then_inc(s_glu_done, 1)
                elif kind == "aout":
                    t = 2 * ((i + 2) % 4)
                    two = sgb[:, t:t + 2, :]
                    v.tensor_tensor(two, two, bank[:], ALU.mult).then_inc(free, 1)
                    evacuated(dve, B, L, kind, i)
                    dve.wait_ge(s_glu_done, DT * (L + 1))
                    v.tensor_tensor(hf[:, t:t + 2, :], sga[:, t:t + 2, :], two, ALU.add).then_inc(s_hf_done, 2)
                    for t in ((4, 5), (6, 7), (), (0, 1, 2, 3))[i]:
                        low_h(n, t, first=2 * ((i + 2) % 4) if i < 2 else 2)
                elif kind == "mout":
                    v.tensor_copy(hf[:, 2 * i:2 * i + 2, :], bank[:]).then_inc(free, 1)

        @block.gpsimd
        def _(pool):
            v = nc.gpsimd

            def low_g(g, slot):
                pool.wait_ge(s_ghi_done, g + 1)
                v.tensor_tensor(g_lo[:, slot, :], hid[:, g % 2, :], g_hi[:, slot, :].bitcast(F32), ALU.subtract)\
                    .then_inc(s_glo_done, 1)

            pool.wait_ge(con_in, 16)
            pool.wait_ge(p1_ld, 16)
            for B, L, kind, i, n in NUMBERED:
                if kind == "gates":
                    pool.wait_ge(s_gates_done, L + 1)
                    for r in range(8):
                        v.tensor_scalar(lts[:, r, :], ident, sm["beta"][:, r:r + 1], None, ALU.mult)\
                            .then_inc(s_pool_db, 1)
                elif kind == "decay":
                    for c in range(TT):
                        pool.wait_ge(s_dec_done, 2 * L + c + 1)
                        four = dec[:, 4 * c:4 * c + 4, :]
                        v.tensor_tensor(four, four, triu.unsqueeze(1).to_broadcast([P, 4, P]), ALU.mult)\
                            .then_inc(s_decm_done, 1)
                elif kind == "qknorm":
                    pool.wait_ge(s_qk_ready, 4 * L + 2)
                    pool.wait_ge(s_silu_done, 6 * (L + 1))
                    pool.wait_ge(s_egr_done, L + 1)
                    v.tensor_tensor(qdec, qT[:, :, P:T], egr.rearrange("p (n t) -> p n t", t=P), ALU.mult)\
                        .then_inc(s_qdec_done, 1)
                elif kind in ("kk", "level") and i < 6:
                    lev = 1 if kind == "kk" else i + 1
                    if kind == "level" and i == 0:
                        continue
                    for c in range(TT):
                        pool.wait_ge(s_lt_done, 2 * L + c + 1)
                        if lev > 1:
                            pool.wait_ge(s_pe_t, 12 * L + 2 * (lev - 2) + c + 1)
                        v.tensor_tensor(lts[:, 4 * c:4 * c + 4, :], lt[:, 4 * c:4 * c + 4, :],
                                        c_("m", lev * P, (lev + 1) * P).unsqueeze(1).to_broadcast([P, 4, P]), ALU.mult)\
                            .then_inc(s_pool_lts, 1)
                elif kind == "gu":
                    low_g(n["g"], i % 4)
                elif kind == "gelu":
                    for t in range(4):
                        low_g(n["g"] + t, t)
                elif kind == "ssm":
                    k = ST * L + i
                    if i == 0:
                        pool.wait_ge(s_tab_arg, k + 1)
                        v.tensor_tensor(Bx["arg"], Bx["arg"], Bx["rnd"], ALU.subtract).then_inc(s_tab_frac, 1)
                    if i + 1 < ST:
                        pool.wait_ge(s_tab_arg, k + 2)
                        v.tensor_tensor(Bx["arg"], Bx["arg"], Bx["rnd"], ALU.subtract).then_inc(s_tab_frac, 1)
                    pool.wait_ge(s_wv_done, 2 * (k + 1))
                    if 2 * k > 0:
                        pool.wait_ge(s_s_sum, 2 * k)
                    v.tensor_tensor(Bx["pc"], tab[:, i % 2, 256:768], wv[:, i % 2, :], ALU.mult).then_inc(s_ab_done, 1)
                    v.tensor_tensor(Bx["pd"], tab[:, i % 2, 0:512], wv[:, i % 2, :], ALU.mult).then_inc(s_ab_done, 1)
                    pool.wait_ge(s_ab_done, 2 * (k + 1))
                    if k - 1 > 0:
                        pool.wait_ge(s_pe_y, k - 1)
                    v.tensor_tensor(sst[:, i % 2, 0:T], Bx["pc"][:, 0:T], Bx["pc"][:, T:2 * T], ALU.subtract)\
                        .then_inc(s_s_sum, 1)
                    v.tensor_tensor(sst[:, i % 2, T:2 * T], Bx["pd"][:, 0:T], Bx["pd"][:, T:2 * T], ALU.add)\
                        .then_inc(s_s_sum, 1)


def kernel(**inputs):
    import concourse.bacc as bacc
    from concourse.bass_utils import run_bass_kernel_spmd

    a = {k: np.asarray(v) for k, v in inputs.items()}
    f32 = np.float32

    def unit_of_columns(w_, c0):
        return w_[:, c0:c0 + P].reshape(DT, P, P).transpose(1, 0, 2).reshape(P, UNIT)

    def unit_of_two(w_, c0, c1):
        both = np.stack([w_[:, c0:c0 + P], w_[:, c1:c1 + P]])
        return both.reshape(2, 4, P, P).transpose(2, 0, 1, 3).reshape(P, UNIT)

    units = []
    ffn = 0
    for B, L, kind, i in STEPS:
        if kind == "pre":
            ffn = i // 2
        if B == 1:
            gate, up, down = a["ffn_w_gate"][L], a["ffn_w_up"][L], a["ffn_w_down"][L]
        else:
            both = a["ffn_w_in_2"][L, ffn]
            gate, up, down = both[:, :FT * P], both[:, FT * P:], a["ffn_w_out_2"][L, ffn]
        if kind == "mod":
            units += [a["mod_w_2"][B - 1][:, (2 * i + e) * P:(2 * i + e + 1) * P].T for e in range(2)]
        elif kind == "pair" and B == 1:
            c0 = 4 * HEADS * HD + 2 * HEADS
            cols = [256 * i, 256 * i + P] if i < 8 else \
                [c0 + 512 + (i - 8) * P, c0 + 1024 + (i - 8) * P] if i < 12 else \
                [c0 + 256 * (i - 12), c0 + 256 * (i - 12) + P]
            units += [unit_of_columns(a["w_in"][L], c) for c in cols]
        elif kind == "pair":
            c0 = 256 * i if i < 8 else 4 * 512 + AH + 256 * (i - 8)
            units += [unit_of_columns(a["mix_w_in_2"][L], c0 + e * P) for e in range(2)]
        elif kind in ("out", "mout"):
            w_ = a["w_out"][L] if kind == "out" else a["mix_w_out_2"][L]
            units += [unit_of_columns(w_, (2 * i + e) * P) for e in range(2)]
        elif kind == "gu":
            units += [unit_of_columns(gate, i * P), unit_of_columns(up, i * P)]
        elif kind == "down":
            units += [down[(2 * i + e) * P:(2 * i + e + 1) * P, :] for e in range(2)]
        elif kind == "aout":
            t = 2 * ((i + 2) % 4)
            units.append(unit_of_two(a["attn_w_out_2"][L], t * P, (t + 1) * P))
        elif kind == "glu":
            units.append(unit_of_two(a["glu_w_2"][L], i * P, D + i * P))
    w = np.stack(units).reshape(-1, 2, P, UNIT).transpose(0, 2, 1, 3).reshape(-1, P, 2 * UNIT)

    def tiles(vec):
        return vec.reshape(-1, P).T

    def rows(vec):
        return np.broadcast_to(vec.reshape(1, -1), (P, vec.size))

    def pack(cols, n, parts):
        out_ = np.zeros((P, n), f32)
        for name, (lo, hi) in cols.items():
            out_[:, lo:hi] = parts[name]
        return out_

    idx = np.arange(P)
    same = lambda size: (idx[:, None] // size) == (idx[None, :] // size)
    masks = [same(2 * z) & ~same(z) & (idx[:, None] < idx[None, :]) for z in (1, 2, 4, 8, 16, 32, 64)]
    future = np.where(idx[None, :] > idx[:, None], BIG, 0.0)
    const = pack(PC, NC, {
        "ident": np.eye(P), "triu": (idx[:, None] <= idx[None, :]), "ones": np.ones((P, P)),
        "m": np.concatenate(masks, axis=1), "pen": np.concatenate([np.zeros((P, P)), future, future], axis=1),
        "time": np.broadcast_to(np.arange(T)[None, :], (P, T)), "c": tiles(a["c_2"][0]),
        "final": tiles(a["final_norm_g"])})

    w_in = a["w_in"]
    lo = 4 * HEADS * HD
    p1 = np.stack([pack(P1, N1, {
        "norm1": tiles(a["norm1_g"][L]), "norm2": tiles(a["norm2_g"][L]),
        "conv": a["dn_conv_w"][L].reshape(TAPS, 12, P).transpose(2, 1, 0).reshape(P, -1),
        "sconv": a["sc_conv_w"][L].reshape(STAPS, 4, P).transpose(2, 1, 0).reshape(P, -1),
        "dn_g": tiles(a["dn_norm_g"][L]), "sc_g": tiles(a["sc_norm_g"][L]),
        "w_ba": w_in[L][:, lo:lo + 8].reshape(DT, P, 8).transpose(1, 0, 2).reshape(P, -1),
        "dt_bias": rows(a["dn_dt_bias"][L]), "a_log": rows(a["dn_a_log"][L]),
        "mod_b": tiles(a["mod_b_2"][L])}) for L in range(LAYERS)], axis=1)

    def ssm_b(b):
        out_ = np.zeros((P, 4, P), f32)
        for ut in range(4):
            for j in range(4):
                for g in range(2):
                    out_[32 * j + 16 * g:32 * j + 16 * g + 16, ut, 64 * g:64 * g + 64] = b[ut * 8 + 2 * j + g].T
        return out_.reshape(P, -1)

    def ssm_c(c):
        out_ = np.zeros((P, ST, 32), f32)
        for st in range(ST):
            for g in range(2):
                out_[64 * g:64 * g + 64, st, 16 * g:16 * g + 16] = c[2 * st + g].T
        return out_.reshape(P, -1)

    p2 = np.stack([pack(P2, N2, {
        "pre": tiles(a["norm_pre_2"][L].reshape(-1)), "post": tiles(a["norm_post_2"][L].reshape(-1)),
        "w_f": a["mix_w_in_2"][L][:, 2048:2056].reshape(DT, P, 8).transpose(1, 0, 2).reshape(P, -1),
        "f_b": rows(a["forget_b_2"][L]), "a_re": tiles(a["ssm_a_re_2"][L].reshape(-1)),
        "a_im": tiles(a["ssm_a_im_2"][L].reshape(-1)), "log_dt": tiles(np.repeat(a["ssm_log_dt_2"][L], SP_)),
        "d": tiles(a["ssm_d_2"][L]), "b_re": ssm_b(a["ssm_b_re_2"][L]), "b_im": ssm_b(a["ssm_b_im_2"][L]),
        "c_re": ssm_c(a["ssm_c_re_2"][L]), "c_im": ssm_c(a["ssm_c_im_2"][L])}) for L in range(LAYERS)], axis=1)

    def feature_major(m):
        return m.T.reshape(DT, P, T).transpose(1, 0, 2)

    ins = {"w": w, "x_in": feature_major(a["x"][0]), "const_in": const, "p1_in": p1, "p2_in": p2}
    ins = {k: np.ascontiguousarray(v) for k, v in ins.items()}
    nc = bacc.Bacc("TRN2", target_bir_lowering=False, num_devices=1)
    aps = [nc.dram_tensor(k, v.shape, F32, kind="ExternalInput").ap() for k, v in ins.items()]
    out = nc.dram_tensor("out", (P, DT, T), F32, kind="ExternalOutput").ap()
    build(nc, *aps, out)
    res = run_bass_kernel_spmd(nc, [ins], core_ids=[0]).results[0]["out"]
    return np.ascontiguousarray(res.transpose(1, 0, 2).reshape(D, T).T)[None]
```
